# Optimizing a Trainium2 kernel written in Bass

```python
import jax, jax.numpy as jnp
from jax import lax
import numpy as np
import math

D_MODEL = 1024
BATCH = 1
SEQ = 256
DEPTH = 2

CHUNK = 64
Q_BLOCK = 128
N_A_LAYERS = (DEPTH + 1) // 2
N_B_LAYERS = DEPTH - N_A_LAYERS
A_HEADS = 16
A_HEAD_DIM = D_MODEL // A_HEADS
B_HEADS = 16
NOPE_DIM = 64
ROPE_DIM = 32
V_DIM = 64
Q_RANK = 768
KV_RANK = 256
ROPE_THETA = 10000.0
N_EXPERTS = 16
N_GROUPS = 4
EXPERTS_PER_GROUP = N_EXPERTS // N_GROUPS
GROUP_SCORE_TOP = 2
TOP_K = 2
D_EXPERT = 512
EPS = 1e-6


def rmsnorm(x, g):
    xf = x.astype(jnp.float32)
    y = xf * lax.rsqrt(jnp.mean(xf * xf, axis=-1, keepdims=True) + EPS)
    return y.astype(x.dtype) * g

def modulate(h, shift, scale):
    return h * (1 + scale[:, None, :]) + shift[:, None, :]

def rope_tables(positions, dtype):
    half = ROPE_DIM // 2
    inv_freq = ROPE_THETA ** (-jnp.arange(half, dtype=jnp.float32) / half)
    ang = positions.astype(jnp.float32)[..., None] * inv_freq
    return jnp.cos(ang).astype(dtype), jnp.sin(ang).astype(dtype)

def apply_rope(x, cos, sin):
    x1, x2 = jnp.split(x, 2, axis=-1)
    return jnp.concatenate([x1 * cos - x2 * sin, x2 * cos + x1 * sin], axis=-1)

def block_sweep(attend, seq):
    return jnp.concatenate([attend(i * Q_BLOCK, (i + 1) * Q_BLOCK) for i in range(seq // Q_BLOCK)], axis=1)

def forgetting_attention(h, w_in, b_f, w_o):
    B, S, D = h.shape
    proj = h @ w_in
    q, k, v, f_logit = jnp.split(proj, [D, 2 * D, 3 * D], axis=-1)
    q = q.reshape(B, S, A_HEADS, A_HEAD_DIM)
    k = k.reshape(B, S, A_HEADS, A_HEAD_DIM)
    v = v.reshape(B, S, A_HEADS, A_HEAD_DIM)
    log_f = jax.nn.log_sigmoid((f_logit + b_f).astype(jnp.float32))
    cum = jnp.cumsum(log_f, axis=1).transpose(0, 2, 1)
    scale = A_HEAD_DIM ** -0.5
    pos = jnp.arange(S)

    def attend(t0, t1):
        s = jnp.einsum('bqhd,bkhd->bhqk', q[:, t0:t1], k[:, :t1], preferred_element_type=jnp.float32) * scale
        s = s + cum[:, :, t0:t1, None] - cum[:, :, None, :t1]
        allowed = pos[t0:t1, None] >= pos[None, :t1]
        p = jax.nn.softmax(jnp.where(allowed, s, -jnp.inf), axis=-1)
        return jnp.einsum('bhqk,bkhd->bqhd', p.astype(v.dtype), v[:, :t1])

    o = block_sweep(attend, S).reshape(B, S, D)
    return o @ w_o

def mla_shared_kv(x, c_act, norm_g, w_mod, b_mod, w_down, latent_g, w_up, cos, sin):
    B, S, _ = x.shape
    shift, scale = jnp.split(c_act @ w_mod + b_mod, 2, axis=-1)
    h = modulate(rmsnorm(x, norm_g), shift, scale)
    c_kv, k_rope = jnp.split(h @ w_down, [KV_RANK], axis=-1)
    c_kv = rmsnorm(c_kv, latent_g)
    kv = (c_kv @ w_up).reshape(B, S, B_HEADS, NOPE_DIM + V_DIM)
    k_nope, v = jnp.split(kv, [NOPE_DIM], axis=-1)
    k_rope = apply_rope(k_rope, cos, sin)
    return k_nope, k_rope, v

def latent_attention(h, k_nope, k_rope, v, w_dq, q_g, w_uq, w_o, cos, sin):
    B, S, _ = h.shape
    cq = rmsnorm(h @ w_dq, q_g)
    q = (cq @ w_uq).reshape(B, S, B_HEADS, NOPE_DIM + ROPE_DIM)
    q_nope, q_rope = jnp.split(q, [NOPE_DIM], axis=-1)
    q_rope = apply_rope(q_rope, cos[:, :, None, :], sin[:, :, None, :])
    scale = (NOPE_DIM + ROPE_DIM) ** -0.5
    chunk_id = jnp.arange(S) // CHUNK

    def attend(t0, t1):
        s = jnp.einsum('bqhd,bkhd->bhqk', q_nope[:, t0:t1], k_nope[:, :t1], preferred_element_type=jnp.float32)
        s = s + jnp.einsum('bqhr,bkr->bhqk', q_rope[:, t0:t1], k_rope[:, :t1], preferred_element_type=jnp.float32)
        allowed = chunk_id[t0:t1, None] >= chunk_id[None, :t1]
        p = jax.nn.softmax(jnp.where(allowed, s * scale, -jnp.inf), axis=-1)
        return jnp.einsum('bhqk,bkhd->bqhd', p.astype(v.dtype), v[:, :t1])

    o = block_sweep(attend, S).reshape(B, S, B_HEADS * V_DIM)
    return o @ w_o

def grouped_moe(h, router_w, router_bias, w_gate, w_up, w_down):
    B, S, D = h.shape
    hf = h.reshape(-1, D)
    n = hf.shape[0]
    scores = jax.nn.sigmoid(jnp.matmul(hf, router_w, preferred_element_type=jnp.float32))
    sel = (scores + router_bias.astype(jnp.float32)).reshape(n, N_GROUPS, EXPERTS_PER_GROUP)
    group_score = lax.top_k(sel, GROUP_SCORE_TOP)[0].sum(-1)
    g = jnp.argmax(group_score, axis=-1)
    g_idx = jnp.broadcast_to(g[:, None, None], (n, 1, EXPERTS_PER_GROUP))
    in_group = jnp.take_along_axis(sel, g_idx, axis=1)[:, 0]
    _, local = lax.top_k(in_group, TOP_K)
    idx = g[:, None] * EXPERTS_PER_GROUP + local
    w = jnp.take_along_axis(scores, idx, axis=1)
    w = w / jnp.sum(w, axis=-1, keepdims=True)
    combine = jnp.sum(jax.nn.one_hot(idx, N_EXPERTS, dtype=jnp.float32) * w[..., None], axis=1).astype(h.dtype)
    y = jnp.zeros_like(hf)
    for e in range(N_EXPERTS):
        a = jax.nn.silu(hf @ w_gate[e]) * (hf @ w_up[e])
        y = y + combine[:, e:e + 1] * (a @ w_down[e])
    return y.reshape(B, S, D)

def first_inputs(seed: int = 0) -> dict:
    key = jax.random.key(seed)
    ks = iter(jax.random.split(key, 40))
    f32 = jnp.float32
    D = D_MODEL

    def w(shape, fan_in, gain=1.0):
        return gain * fan_in ** -0.5 * jax.random.normal(next(ks), shape, f32)

    def gain(shape):
        return 1.0 + 0.05 * jax.random.normal(next(ks), shape, f32)

    def small(shape, s):
        return s * jax.random.normal(next(ks), shape, f32)

    x = jax.random.normal(next(ks), (BATCH, SEQ, D), f32)
    c = jax.random.normal(next(ks), (BATCH, D), f32)
    offset = jax.random.randint(next(ks), (BATCH, 1), 0, 4096, dtype=jnp.int32)
    positions = (jnp.arange(SEQ, dtype=jnp.int32)[None, :] + offset).astype(jnp.int32)
    return {
        "x": x,
        "c": c,
        "positions": positions,
        "a_norm_g": gain((N_A_LAYERS, D)),
        "a_w_in": w((N_A_LAYERS, D, 3 * D + A_HEADS), D),
        "a_b_f": jax.random.uniform(next(ks), (N_A_LAYERS, A_HEADS), f32, 1.0, 5.0),
        "a_w_o": w((N_A_LAYERS, D, D), D),
        "kv_norm_g": gain((D,)),
        "kv_w_mod": w((D, 2 * D), D, 0.5),
        "kv_b_mod": small((2 * D,), 0.02),
        "kv_w_down": w((D, KV_RANK + ROPE_DIM), D),
        "kv_latent_g": gain((KV_RANK,)),
        "kv_w_up": w((KV_RANK, B_HEADS * (NOPE_DIM + V_DIM)), KV_RANK),
        "b_norm_g": gain((N_B_LAYERS, D)),
        "b_w_dq": w((N_B_LAYERS, D, Q_RANK), D),
        "b_q_norm_g": gain((N_B_LAYERS, Q_RANK)),
        "b_w_uq": w((N_B_LAYERS, Q_RANK, B_HEADS * (NOPE_DIM + ROPE_DIM)), Q_RANK),
        "b_w_o": w((N_B_LAYERS, B_HEADS * V_DIM, D), B_HEADS * V_DIM),
        "w_mod": w((DEPTH, D, 6 * D), D, 0.5),
        "b_mod": small((DEPTH, 6 * D), 0.02),
        "ffn_norm_g": gain((DEPTH, D)),
        "router_w": w((D, N_EXPERTS), D),
        "router_bias": small((N_EXPERTS,), 0.01),
        "exp_w_gate": w((DEPTH, N_EXPERTS, D, D_EXPERT), D),
        "exp_w_up": w((DEPTH, N_EXPERTS, D, D_EXPERT), D),
        "exp_w_down": w((DEPTH, N_EXPERTS, D_EXPERT, D), D_EXPERT),
        "final_norm_g": gain((D,)),
    }

def first_block(x, c, positions, a_norm_g, a_w_in, a_b_f, a_w_o, kv_norm_g, kv_w_mod, kv_b_mod,
              kv_w_down, kv_latent_g, kv_w_up, b_norm_g, b_w_dq, b_q_norm_g, b_w_uq, b_w_o,
              w_mod, b_mod, ffn_norm_g, router_w, router_bias, exp_w_gate, exp_w_up, exp_w_down,
              final_norm_g):
    c_act = jax.nn.silu(c)
    cos, sin = rope_tables(positions, x.dtype)
    shared_kv = None
    for layer in range(DEPTH):
        sh1, sc1, g1, sh2, sc2, g2 = jnp.split(c_act @ w_mod[layer] + b_mod[layer], 6, axis=-1)
        if layer < N_A_LAYERS:
            h = modulate(rmsnorm(x, a_norm_g[layer]), sh1, sc1)
            mix = forgetting_attention(h, a_w_in[layer], a_b_f[layer], a_w_o[layer])
        else:
            j = layer - N_A_LAYERS
            h = modulate(rmsnorm(x, b_norm_g[j]), sh1, sc1)
            k_nope, k_rope, v = shared_kv
            mix = latent_attention(h, k_nope, k_rope, v, b_w_dq[j], b_q_norm_g[j], b_w_uq[j], b_w_o[j], cos, sin)
        x = x + g1[:, None, :] * mix
        h = modulate(rmsnorm(x, ffn_norm_g[layer]), sh2, sc2)
        x = x + g2[:, None, :] * grouped_moe(h, router_w, router_bias, exp_w_gate[layer], exp_w_up[layer], exp_w_down[layer])
        if layer == N_A_LAYERS - 1:
            shared_kv = mla_shared_kv(x, c_act, kv_norm_g, kv_w_mod, kv_b_mod, kv_w_down, kv_latent_g, kv_w_up, cos, sin)
    return rmsnorm(x, final_norm_g)


DEPTH_2 = 4

N_MIXERS = 3
N_RET = (DEPTH_2 + 2) // 3
N_MOBA = (DEPTH_2 + 1) // 3
N_DIFF = DEPTH_2 // 3

RET_HEADS = 4
RET_DK = D_MODEL // RET_HEADS
RET_DV = 2 * RET_DK
RET_CHUNK = 128
ROPE_BASE = 10000.0

ATTN_HEADS = 16
HEAD_DIM = D_MODEL // ATTN_HEADS
MOBA_BLOCK = 256
MOBA_TOPK = 3
MOBA_Q_CHUNK = 16
DIFF_HEADS = ATTN_HEADS // 2
DIFF_V_DIM = 2 * HEAD_DIM
ATTN_Q_BLOCK = 128

REL_BUCKETS = 32
REL_MAX_EXACT = REL_BUCKETS // 2
REL_MAX_DISTANCE = 1024

D_FF = 4 * D_MODEL
NEG = -1e30


def _rmsnorm(x, w):
    xf = x.astype(jnp.float32)
    y = xf * lax.rsqrt(jnp.mean(xf * xf, axis=-1, keepdims=True) + EPS)
    return y.astype(x.dtype) * w

def _rel_bucket(dist):
    n = jnp.maximum(dist, 0)
    nf = jnp.maximum(n, 1).astype(jnp.float32)
    large = REL_MAX_EXACT + (jnp.log(nf / REL_MAX_EXACT) / math.log(REL_MAX_DISTANCE / REL_MAX_EXACT)
                             * (REL_BUCKETS - REL_MAX_EXACT)).astype(jnp.int32)
    large = jnp.minimum(large, REL_BUCKETS - 1)
    return jnp.where(n < REL_MAX_EXACT, n, large)

def _rotary(x):
    S, d = x.shape[2], x.shape[3]
    inv_freq = ROPE_BASE ** (-jnp.arange(0, d, 2, dtype=jnp.float32) / d)
    ang = jnp.arange(S, dtype=jnp.float32)[:, None] * inv_freq[None, :]
    cos, sin = jnp.cos(ang), jnp.sin(ang)
    x1, x2 = x[..., : d // 2], x[..., d // 2:]
    return jnp.concatenate([x1 * cos - x2 * sin, x1 * sin + x2 * cos], axis=-1)

def _squared_relu_mlp(h, w_up, w_down):
    u = jax.nn.relu(h @ w_up)
    return (u * u) @ w_down

def _retention_mixer(h, w_in, w_out):
    B, S, _ = h.shape
    H, dk, dv, C = RET_HEADS, RET_DK, RET_DV, RET_CHUNK
    N = S // C
    proj = (h @ w_in).astype(jnp.float32)
    q, k, v, g = jnp.split(proj, [H * dk, 2 * H * dk, 2 * H * dk + H * dv], axis=-1)
    q = _rotary(q.reshape(B, S, H, dk).transpose(0, 2, 1, 3))
    k = _rotary(k.reshape(B, S, H, dk).transpose(0, 2, 1, 3)) * (dk ** -0.5)
    v = v.reshape(B, S, H, dv).transpose(0, 2, 1, 3)

    log_gamma = jnp.log(1.0 - 2.0 ** (-5.0 - jnp.arange(H, dtype=jnp.float32)))
    pos = jnp.arange(C, dtype=jnp.float32)
    rel = pos[:, None] - pos[None, :]
    inner_decay = jnp.where(rel >= 0, jnp.exp(jnp.maximum(rel, 0.0)[None] * log_gamma[:, None, None]), 0.0)

    qc = q.reshape(B, H, N, C, dk)
    kc = k.reshape(B, H, N, C, dk)
    vc = v.reshape(B, H, N, C, dv)
    s_in = jnp.einsum('bhnid,bhnjd->bhnij', qc, kc) * inner_decay[:, None]
    inner = jnp.einsum('bhnij,bhnjv->bhniv', s_in, vc)
    q_dec = qc * jnp.exp((pos + 1.0)[None, :] * log_gamma[:, None])[:, None, :, None]
    k_dec = kc * jnp.exp((C - 1.0 - pos)[None, :] * log_gamma[:, None])[:, None, :, None]
    chunk_decay = jnp.exp(C * log_gamma)[:, None, None]

    def step(state, xs):
        qn, kn, vn = xs
        out = jnp.einsum('bhid,bhdv->bhiv', qn, state)
        state = state * chunk_decay + jnp.einsum('bhjd,bhjv->bhdv', kn, vn)
        return state, out

    xs = (jnp.moveaxis(q_dec, 2, 0), jnp.moveaxis(k_dec, 2, 0), jnp.moveaxis(vc, 2, 0))
    _, cross = lax.scan(step, jnp.zeros((B, H, dk, dv), jnp.float32), xs)
    o = (inner + jnp.moveaxis(cross, 0, 2)).reshape(B, H, S, dv)
    o = o * lax.rsqrt(jnp.mean(o * o, axis=-1, keepdims=True) + EPS)
    o = o.transpose(0, 2, 1, 3).reshape(B, S, H * dv)
    return ((jax.nn.silu(g) * o) @ w_out).astype(h.dtype)

def _moba_mixer(h, w_in, q_norm_w, k_norm_w, w_out, rel_bias):
    B, S, _ = h.shape
    H, d, BS, QC = ATTN_HEADS, HEAD_DIM, MOBA_BLOCK, MOBA_Q_CHUNK
    proj = h @ w_in
    q, k, v = jnp.split(proj, 3, axis=-1)
    q = _rmsnorm(q.reshape(B, S, H, d), q_norm_w).transpose(0, 2, 1, 3).astype(jnp.float32) * (d ** -0.5)
    k = _rmsnorm(k.reshape(B, S, H, d), k_norm_w).transpose(0, 2, 1, 3).astype(jnp.float32)
    v = v.reshape(B, S, H, d).transpose(0, 2, 1, 3)
    NB = -(-S // BS)
    pad = NB * BS - S
    k_pad = jnp.pad(k, ((0, 0), (0, 0), (0, pad), (0, 0)))
    v_pad = jnp.pad(v, ((0, 0), (0, 0), (0, pad), (0, 0)))
    kb = k_pad.reshape(B, H, NB, BS, d)
    vb = v_pad.reshape(B, H, NB, BS, d)
    k_mean = kb.mean(axis=3)
    topk = min(MOBA_TOPK, NB)
    bias_t = rel_bias.T.astype(jnp.float32)
    head_idx = jnp.arange(H)[None, :, None, None, None]
    in_block = jnp.arange(BS)
    gather = jax.vmap(jax.vmap(lambda blocks, ix: blocks[ix]))

    def chunk(c):
        t0 = c * QC
        b = t0 // BS
        t = t0 + jnp.arange(QC)
        qc = lax.dynamic_slice_in_dim(q, t0, QC, axis=2)
        gate = jnp.einsum('bhqd,bhnd->bhqn', qc, k_mean)
        gate = jnp.where(jnp.arange(NB) < b, gate, NEG)
        _, idx = lax.top_k(gate, topk)
        valid = idx < b
        k_sel = gather(kb, idx)
        v_sel = gather(vb, idx)
        s_sel = jnp.einsum('bhqd,bhqkjd->bhqkj', qc, k_sel)
        kpos = idx[..., None] * BS + in_block
        s_sel = s_sel + bias_t[head_idx, _rel_bucket(t[:, None, None] - kpos)]
        s_sel = jnp.where(valid[..., None], s_sel, NEG)
        k_own = lax.dynamic_slice_in_dim(k_pad, b * BS, BS, axis=2)
        v_own = lax.dynamic_slice_in_dim(v_pad, b * BS, BS, axis=2)
        dist = t[:, None] - (b * BS + in_block)[None, :]
        s_own = jnp.einsum('bhqd,bhjd->bhqj', qc, k_own) + bias_t[:, _rel_bucket(dist)]
        s_own = jnp.where(dist >= 0, s_own, NEG)
        scores = jnp.concatenate([s_sel.reshape(B, H, QC, topk * BS), s_own], axis=-1)
        p = jax.nn.softmax(scores, axis=-1)
        p_sel = p[..., : topk * BS].reshape(B, H, QC, topk, BS)
        p_own = p[..., topk * BS:]
        return (jnp.einsum('bhqkj,bhqkjd->bhqd', p_sel, v_sel)
                + jnp.einsum('bhqj,bhjd->bhqd', p_own, v_own))

    outs = lax.map(chunk, jnp.arange(S // QC))
    o = outs.transpose(1, 2, 0, 3, 4).reshape(B, H, S, d).transpose(0, 2, 1, 3).reshape(B, S, H * d)
    return (o @ w_out).astype(h.dtype)

def _diff_mixer(h, w_in, q_norm_w, k_norm_w, lambdas, subln_w, w_out, rel_bias, lambda_init):
    B, S, _ = h.shape
    H2, d, QB = 2 * DIFF_HEADS, HEAD_DIM, ATTN_Q_BLOCK
    proj = h @ w_in
    q, k, v = jnp.split(proj, 3, axis=-1)
    q = _rmsnorm(q.reshape(B, S, H2, d), q_norm_w).transpose(0, 2, 1, 3).astype(jnp.float32) * (d ** -0.5)
    k = _rmsnorm(k.reshape(B, S, H2, d), k_norm_w).transpose(0, 2, 1, 3).astype(jnp.float32)
    v = v.reshape(B, S, DIFF_HEADS, DIFF_V_DIM).transpose(0, 2, 1, 3)
    lam = lambdas.astype(jnp.float32)
    lambda_full = jnp.exp(jnp.sum(lam[0] * lam[1])) - jnp.exp(jnp.sum(lam[2] * lam[3])) + lambda_init
    bias_t = rel_bias.T.astype(jnp.float32)
    kpos = jnp.arange(S)

    def block(c):
        t0 = c * QB
        t = t0 + jnp.arange(QB)
        qb = lax.dynamic_slice_in_dim(q, t0, QB, axis=2)
        dist = t[:, None] - kpos[None, :]
        s = jnp.einsum('bhqd,bhkd->bhqk', qb, k) + bias_t[:, _rel_bucket(dist)]
        s = jnp.where(dist >= 0, s, NEG)
        p = jax.nn.softmax(s, axis=-1).reshape(B, DIFF_HEADS, 2, QB, S)
        attn = p[:, :, 0] - lambda_full * p[:, :, 1]
        return jnp.einsum('bhqk,bhkv->bhqv', attn, v)

    outs = lax.map(block, jnp.arange(S // QB))
    o = outs.transpose(1, 2, 0, 3, 4).reshape(B, DIFF_HEADS, S, DIFF_V_DIM)
    o = _rmsnorm(o, subln_w) * (1.0 - lambda_init)
    o = o.transpose(0, 2, 1, 3).reshape(B, S, DIFF_HEADS * DIFF_V_DIM)
    return (o @ w_out).astype(h.dtype)

def second_inputs(seed: int = 0) -> dict:
    key = jax.random.key(seed)
    ks = jax.random.split(key, 18)

    def nrm(k, shape, scale):
        return jax.random.normal(k, shape, jnp.float32) * scale

    D = D_MODEL
    ret_in = 2 * RET_HEADS * RET_DK + 2 * RET_HEADS * RET_DV
    return {
        "x": nrm(ks[0], (BATCH, SEQ, D), 1.0),
        "rel_bias": nrm(ks[1], (REL_BUCKETS, ATTN_HEADS), 0.5),
        "norm1": 1.0 + nrm(ks[2], (DEPTH_2, D), 0.02),
        "norm2": 1.0 + nrm(ks[3], (DEPTH_2, D), 0.02),
        "w_up": nrm(ks[4], (DEPTH_2, D, D_FF), D ** -0.5),
        "w_down": nrm(ks[5], (DEPTH_2, D_FF, D), D_FF ** -0.5),
        "ret_w_in": nrm(ks[6], (N_RET, D, ret_in), D ** -0.5),
        "ret_w_out": nrm(ks[7], (N_RET, RET_HEADS * RET_DV, D), (RET_HEADS * RET_DV) ** -0.5),
        "moba_w_in": nrm(ks[8], (N_MOBA, D, 3 * ATTN_HEADS * HEAD_DIM), D ** -0.5),
        "moba_q_norm": 1.0 + nrm(ks[9], (N_MOBA, HEAD_DIM), 0.02),
        "moba_k_norm": 1.0 + nrm(ks[10], (N_MOBA, HEAD_DIM), 0.02),
        "moba_w_out": nrm(ks[11], (N_MOBA, ATTN_HEADS * HEAD_DIM, D), (ATTN_HEADS * HEAD_DIM) ** -0.5),
        "diff_w_in": nrm(ks[12], (N_DIFF, D, 3 * ATTN_HEADS * HEAD_DIM), D ** -0.5),
        "diff_q_norm": 1.0 + nrm(ks[13], (N_DIFF, HEAD_DIM), 0.02),
        "diff_k_norm": 1.0 + nrm(ks[14], (N_DIFF, HEAD_DIM), 0.02),
        "diff_lambda": nrm(ks[15], (N_DIFF, 4, HEAD_DIM), 0.1),
        "diff_subln": 1.0 + nrm(ks[16], (N_DIFF, DIFF_V_DIM), 0.02),
        "diff_w_out": nrm(ks[17], (N_DIFF, DIFF_HEADS * DIFF_V_DIM, D), (DIFF_HEADS * DIFF_V_DIM) ** -0.5),
    }

def second_block(x, rel_bias, norm1, norm2, w_up, w_down, ret_w_in, ret_w_out,
              moba_w_in, moba_q_norm, moba_k_norm, moba_w_out,
              diff_w_in, diff_q_norm, diff_k_norm, diff_lambda, diff_subln, diff_w_out):
    for i in range(DEPTH_2):
        kind, j = i % N_MIXERS, i // N_MIXERS
        h = _rmsnorm(x, norm1[i])
        if kind == 0:
            m = _retention_mixer(h, ret_w_in[j], ret_w_out[j])
        elif kind == 1:
            m = _moba_mixer(h, moba_w_in[j], moba_q_norm[j], moba_k_norm[j], moba_w_out[j], rel_bias)
        else:
            lambda_init = 0.8 - 0.6 * math.exp(-0.3 * i)
            m = _diff_mixer(h, diff_w_in[j], diff_q_norm[j], diff_k_norm[j], diff_lambda[j],
                            diff_subln[j], diff_w_out[j], rel_bias, lambda_init)
        x = x + m
        x = x + _squared_relu_mlp(_rmsnorm(x, norm2[i]), w_up[i], w_down[i])
    return x


def setup_inputs(seed=0):
    out = dict(first_inputs(seed))
    for name, value in second_inputs(seed + 1).items():
        if name != "x":
            out[name + "_2"] = value
    return out


def reference(
    x, c, positions, a_norm_g, a_w_in, a_b_f, a_w_o, kv_norm_g, kv_w_mod, kv_b_mod, kv_w_down,
    kv_latent_g, kv_w_up, b_norm_g, b_w_dq, b_q_norm_g, b_w_uq, b_w_o, w_mod, b_mod, ffn_norm_g,
    router_w, router_bias, exp_w_gate, exp_w_up, exp_w_down, final_norm_g, rel_bias_2, norm1_2,
    norm2_2, w_up_2, w_down_2, ret_w_in_2, ret_w_out_2, moba_w_in_2, moba_q_norm_2,
    moba_k_norm_2, moba_w_out_2, diff_w_in_2, diff_q_norm_2, diff_k_norm_2, diff_lambda_2,
    diff_subln_2, diff_w_out_2,
):
    x = first_block(
        x, c, positions, a_norm_g, a_w_in, a_b_f, a_w_o, kv_norm_g, kv_w_mod, kv_b_mod,
        kv_w_down, kv_latent_g, kv_w_up, b_norm_g, b_w_dq, b_q_norm_g, b_w_uq, b_w_o, w_mod,
        b_mod, ffn_norm_g, router_w, router_bias, exp_w_gate, exp_w_up, exp_w_down,
        final_norm_g,
    )
    return second_block(
        x, rel_bias_2, norm1_2, norm2_2, w_up_2, w_down_2, ret_w_in_2, ret_w_out_2, moba_w_in_2,
        moba_q_norm_2, moba_k_norm_2, moba_w_out_2, diff_w_in_2, diff_q_norm_2, diff_k_norm_2,
        diff_lambda_2, diff_subln_2, diff_w_out_2,
    )


_drawn_inputs = setup_inputs


def setup_inputs(seed=0):
    import zlib

    import numpy as np

    out = dict(_drawn_inputs(seed))
    spreads = {}
    factors = {'b_norm_g': 8.0,
     'b_q_norm_g': 8.0,
     'moba_q_norm_2': 8.0,
     'moba_k_norm_2': 8.0,
     'diff_q_norm_2': 8.0,
     'diff_k_norm_2': 8.0,
     'diff_subln_2': 22.395}
    for name, (base, spread) in spreads.items():
        noise = np.random.default_rng([zlib.crc32(name.encode()), seed]).standard_normal(out[name].shape)
        drawn = base * np.exp(spread * noise) if base else spread * noise
        out[name] = __import__('jax').numpy.asarray(drawn.astype(out[name].dtype))
    for name, factor in factors.items():
        out[name] = (out[name] * factor).astype(out[name].dtype)
    return out
```

```python
from contextlib import ExitStack

import numpy as np

import concourse.bass as bass
from concourse import mybir

F32 = mybir.dt.float32
I32 = mybir.dt.int32
ALU = mybir.AluOpType
ACT = mybir.ActivationFunctionType
X = mybir.AxisListType.X

P = 128
S = 256
TB = S // P
D = 1024
KD = D // P
HEADS = 16
HD = D // HEADS
NOPE, ROPE = 64, 32
QK_B = NOPE + ROPE
Q_RANK, KV_RANK = 768, 256
CHUNK_B = 64
EXPERTS, GROUPS = 16, 4
PER_GROUP = EXPERTS // GROUPS
DE = 512
D_FF = 4 * D
FF_PARTS = D_FF // DE
RH, RDK, RDV = 4, 256, 512
RET_IN = 2 * RH * RDK + 2 * RH * RDV
EPS = 1e-6
NEG = -1e30
RING = 4
SLOT = 4096
HALF = SLOT // 2

LAMBDA_INIT = 0.8 - 0.6 * float(np.exp(-0.3 * 2))


def shape_constants():
    f = np.float32
    q = np.arange(P)[:, None]
    c = np.arange(S)[None, :]
    dist = q + P - c
    causal = np.where(dist >= 0, f(0), f(NEG)).astype(f)
    chunked = np.where((q + P) // CHUNK_B >= c // CHUNK_B, f(0), f(NEG)).astype(f)
    ident = np.eye(P, dtype=f)
    upto = (np.arange(P)[:, None] <= np.arange(P)[None, :]).astype(f)
    ones = np.ones((P, P), f)
    lg = np.log(f(1.0) - f(2.0) ** (f(-5.0) - np.arange(RH, dtype=f))).astype(f)
    rel = np.arange(S)[None, :] - np.arange(P)[:, None]
    decay = np.where(rel[:, None, :] >= 0,
                     np.exp(np.maximum(rel, 0).astype(f)[:, None, :] * lg[None, :, None]), f(0)).astype(f)
    decay = decay * f(RDK ** -0.5)
    inv = (f(10000.0) ** (-np.arange(0, RDK, 2, dtype=f) / f(RDK))).astype(f)
    ang = (inv[:, None] * np.arange(S, dtype=f)[None, :]).astype(f)
    half = ROPE // 2
    inv_rope = (f(10000.0) ** (-np.arange(half, dtype=f) / f(half))).astype(f)
    n = (S - 1 - np.arange(S))
    large = 16 + (np.log(np.maximum(n, 1).astype(f) / f(16)) / f(np.log(64.0)) * f(16)).astype(np.int32)
    bucket = np.where(n < 16, n, np.minimum(large, 31))
    onehot = (np.arange(32)[:, None] == bucket[None, :]).astype(f)
    return {
        "squares": np.concatenate([ident, upto, ones], 1),
        "masks": np.concatenate([causal, chunked], 1),
        "decay": np.ascontiguousarray(decay.reshape(P, RH * S)),
        "rotary": np.concatenate([np.cos(ang), np.sin(ang)], 1).astype(f),
        "small": np.tile(np.concatenate([inv_rope, np.array([4, 3, 2, 1], f)])[None, :], (P, 1)),
        "onehot": onehot,
    }


class Use:

    def __init__(self, u, chunk=None, fill=None):
        self.u, self.chunk, self.fill = u, chunk, fill


class Plan:

    def __init__(self):
        self.n = {}
        self.stats = []
        self.streamed = []

    def take(self, what, k=1):
        at = self.n.get(what, 0)
        self.n[what] = at + k
        return at

    def fills(self, k):
        return [Use(self.take("use"), fill=self.take("fill")) for _ in range(k)]

    def chunk(self, *what):
        self.streamed.append(what)
        return self.take("chunk")

    def proj(self, *what):
        return Use(self.take("use"), chunk=self.chunk(*what))

    def stat(self, cols, length):
        self.stats.append((cols, 1.0 / length))
        return self.take("stat")


class Phase:
    pass


def norm_plan(p, after):
    n = Phase()
    n.after, n.stat, n.scaled = after, p.stat(TB, D), p.take("scaled")
    n.uses = p.fills(2)
    return n


def attention_plan(p, wo):
    a = Phase()
    a.kq = p.fills(2 * HEADS // 4)
    a.unit = p.take("unit", 2 * HEADS // 4)
    a.scores = p.fills(2 * HEADS // 4)
    a.oT = p.fills(2)
    a.wo = [p.chunk("rows", wo, j) for j in range(2)]
    a.update = p.take("update")
    return a


def experts_plan(p, layer, mods):
    m = Phase()
    m.norm = norm_plan(p, p.n["update"])
    m.router = p.fills(1)[0]
    m.first = p.take("gated", EXPERTS)
    m.gate, m.up, m.down, m.mod = [], [], [], []
    for e in range(EXPERTS):
        m.gate.append(p.proj("cols", "exp_w_gate", (layer, e), 0))
        m.up.append(p.proj("cols", "exp_w_up", (layer, e), 0))
        if e:
            m.down.append(p.chunk("rows_e", "exp_w_down", (layer, e - 1)))
        if mods:
            m.mod.append(p.proj("cols", *mods[e]))
        if e == 0:
            m.comb = p.fills(EXPERTS // 4)
    m.down.append(p.chunk("rows_e", "exp_w_down", (layer, EXPERTS - 1)))
    m.update = p.take("update")
    return m


def mlp_plan(p, layer):
    m = Phase()
    m.norm = norm_plan(p, p.n["update"])
    m.first = p.take("gated", FF_PARTS)
    m.up, m.down = [], []
    for j in range(FF_PARTS):
        m.up.append(p.proj("cols", "w_up_2", layer, j))
        if j:
            m.down.append(p.chunk("rows", ("w_down_2", layer), j - 1))
    m.down.append(p.chunk("rows", ("w_down_2", layer), FF_PARTS - 1))
    m.update = p.take("update")
    return m


def retention_plan(p, j):
    r = Phase()
    r.norm = norm_plan(p, p.n["update"])
    r.proj = [p.proj("cols", "ret_w_in_2", j, c) for c in range(RET_IN // 512)]
    r.scores = p.fills(RH)
    r.head = p.take("head", RH)
    r.stat = [p.stat(TB, RDV) for _ in range(RH)]
    r.oT = p.fills(4)
    r.wo = [p.chunk("rows", ("ret_w_out_2", j), c) for c in range(RH * RDV // 512)]
    r.update = p.take("update")
    return r


def softmax_layer_plan(p, name, diff):
    a = Phase()
    a.norm = norm_plan(p, p.n["update"])
    a.proj = [p.proj("cols", name + "_w_in_2", 0, c) for c in range(6)]
    a.qk_stat = [p.stat(TB * HEADS, HD) for _ in range(2)]
    a.qk_normed = p.take("qk_normed", 2)
    a.diff = diff
    att = attention_plan(p, (name + "_w_out_2", 0))
    if diff:
        a.o_stat = p.stat(TB * HEADS // 2, 2 * HD)
    a.att = att
    return a


def make_plan():
    p = Plan()
    p.n["update"] = 0
    p.columns, p.rel = p.fills(2)
    p.mod_a = [p.proj("cols", "w_mod", 0, c) for c in range(4)]
    p.a_norm = norm_plan(p, 0)
    p.f_logit = p.fills(1)[0]
    p.a_proj, p.a_mods = [], []
    c = 4
    for j in range(6):
        p.a_proj.append(p.proj("cols", "a_w_in", 0, j))
        mods = []
        for _ in range(2 if j < 2 else 1):
            mods.append(p.proj("cols", "w_mod", 0, c))
            c += 1
        p.a_mods.append(mods)
        if j == 0:
            p.cum_q = p.fills(1)[0]
            p.cum_k = p.fills(4)
    p.gates_a = p.fills(2)
    p.att_a = attention_plan(p, ("a_w_o", 0))
    mods = [("kv_w_mod", None, c) for c in range(4)] + [("w_mod", 1, c) for c in range(12)]
    p.moe0 = experts_plan(p, 0, mods)
    p.kv_norm = norm_plan(p, p.n["update"])
    p.kv_down = p.proj("kv_down")
    p.kv_stat = p.stat(TB, KV_RANK)
    p.ckvT = p.fills(1)[0]
    p.kv_up = [p.proj("kv_up", j) for j in range(4)]
    p.b_norm = norm_plan(p, p.n["update"])
    p.dq = [p.proj("cols", "b_w_dq", 0, 0), p.proj("dq_tail")]
    p.cq_stat = p.stat(TB, Q_RANK)
    p.cqT = p.fills(2)
    p.uq = [p.proj("uq", j) for j in range(3)]
    p.gates_b = p.fills(2)
    p.att_b = attention_plan(p, ("b_w_o", 0))
    p.moe1 = experts_plan(p, 1, None)
    p.final_stat = p.stat(TB, D)
    p.final_update = p.take("update")
    p.ret0 = retention_plan(p, 0)
    p.mlp0 = mlp_plan(p, 0)
    p.moba = softmax_layer_plan(p, "moba", False)
    p.mlp1 = mlp_plan(p, 1)
    p.diff = softmax_layer_plan(p, "diff", True)
    p.mlp2 = mlp_plan(p, 2)
    p.ret1 = retention_plan(p, 1)
    p.mlp3 = mlp_plan(p, 3)
    return p


def spread(ap, axis, n):
    shape = list(ap.shape)
    return ap.unsqueeze(axis).to_broadcast(shape[:axis] + [n] + shape[axis:])




def build(nc, w, table, out, rel_scratch):
    plan = make_plan()
    ctx = ExitStack()
    with ctx:
        def sb(name, shape, dt=F32):
            return ctx.enter_context(nc.sbuf_tensor(name, shape, dt))

        def sem(name):
            return ctx.enter_context(nc.semaphore(name))

        ring = sb("ring", [P, RING, SLOT])
        x = sb("x", [P, TB, D])
        xn = sb("xn", [P, TB, D])
        hT = sb("hT", [P, KD, S])
        gates = sb("gates", [P, 2, D])
        squares = sb("squares", [P, 3 * P])
        masks = sb("masks", [P, 2 * S])
        decay = sb("decay", [P, RH, S])
        rotary = sb("rotary", [P, 2, S])
        small = sb("small", [P, ROPE // 2 + PER_GROUP])
        cols = sb("cols", [P, 2 * P])
        mod = sb("mod", [P, 112])
        w_f = sb("w_f", [P, KD, HEADS])
        w_router = sb("w_router", [P, KD, EXPERTS])
        head_gain = sb("head_gain", [P, 4])
        subln = sb("subln", [P, 1])
        b_f = sb("b_f", [P, HEADS])
        r_bias = sb("r_bias", [P, EXPERTS])
        c_act = sb("c_act", [P, KD])
        gain = sb("gain", [P, KD])
        ss = sb("ss", [P, 2, 32])
        rs = sb("rs", [P, 2, 32])
        minus_half = sb("minus_half", [P, 32])
        negmax = sb("negmax", [P, 2, 4])
        expsum = sb("expsum", [P, 2, 4])
        recip = sb("recip", [P, 2, 4])
        lam = sb("lam", [P, 8])
        pos_i = sb("pos_i", [P, TB], I32)
        pos_f = sb("pos_f", [P, TB])
        rope = sb("rope", [P, 2, TB, ROPE // 2])
        ropew = sb("ropew", [P, 2, TB, ROPE // 2])
        logf = sb("logf", [P, TB, HEADS])
        logw = sb("logw", [P, TB, HEADS])
        cumq = sb("cumq", [P, TB, HEADS])
        route = sb("route", [P, 10, TB * EXPERTS])
        work = sb("work", [P, 24 * 1024])

        ident, upto_m, ones_m = (squares[:, k * P:(k + 1) * P] for k in range(3))
        causal, chunked = masks[:, 0:S], masks[:, S:2 * S]
        inv_rope, descending = small[:, 0:ROPE // 2], small[:, ROPE // 2:]

        q_area, k_area = work[:, 0:3072], work[:, 3072:6144]
        v_tok = work[:, 6144:8192].rearrange("p (b n) -> p b n", b=TB)
        qT = work[:, 8192:12288].rearrange("p (h t) -> p h t", h=HEADS)
        kT = work[:, 12288:16384].rearrange("p (h t) -> p h t", h=HEADS)
        bias0 = work[:, 16384:18432].rearrange("p (h t) -> p h t", h=HEADS)
        bias1 = work[:, 18432:22528].rearrange("p (h t) -> p h t", h=HEADS)
        relbias = work[:, 16384:20480].rearrange("p (h t) -> p h t", h=HEADS)
        probs = work[:, 0:2048].rearrange("p (s h t) -> p s h t", s=2, h=4)
        diff_tmp = work[:, 2048:2560].rearrange("p (j i d) -> p j i d", j=2, i=2)
        pT = work[:, 3072:5120].rearrange("p (s h t) -> p s h t", s=2, h=4)
        o_tok = work[:, 22528:24576].rearrange("p (b n) -> p b n", b=TB)
        o_flat = work[:, 22528:24576]
        ckv = work[:, 16384:16384 + 576].rearrange("p (b n) -> p b n", b=TB)
        ckvT = work[:, 16960:16960 + 512].rearrange("p (k t) -> p k t", k=2)
        cq = work[:, 17472:17472 + 1536].rearrange("p (b n) -> p b n", b=TB)
        cqT = work[:, 19008:19008 + 1536].rearrange("p (k t) -> p k t", k=6)
        rot = work[:, 22528:24576].rearrange("p (i n) -> p i n", i=4)
        act = work[:, 0:2048].rearrange("p (s f t) -> p s f t", s=2, f=4)
        prod = work[:, 2048:3072].rearrange("p (f t) -> p f t", f=4)
        gated = work[:, 3072:5120].rearrange("p (s f t) -> p s f t", s=2, f=4)
        comb = work[:, 20480:24576].rearrange("p (e t) -> p e t", e=EXPERTS)
        r_qT = work[:, 0:2048].rearrange("p (k t) -> p k t", k=8)
        r_kT = work[:, 2048:4096].rearrange("p (k t) -> p k t", k=8)
        r_v = work[:, 4096:8192].rearrange("p (b n) -> p b n", b=TB)
        r_g = work[:, 8192:12288].rearrange("p (b n) -> p b n", b=TB)
        r_o = work[:, 12288:16384].rearrange("p (b n) -> p b n", b=TB)
        r_oT = work[:, 16384:20480].rearrange("p (k t) -> p k t", k=16)
        r_tmp = work[:, 20480:21504].rearrange("p (i h t) -> p i h t", i=2, h=2)
        r_s = work[:, 22528:22528 + 768].rearrange("p (s t) -> p s t", s=2)
        rows = work[:, 0:256]
        rel_in = work[0:32, 256:256 + 16]
        onehot = work[0:32, 512:512 + 256]
        rel_rows = work[0:16, 1024:1024 + 384]
        lam_in = work[:, 2048:2048 + 256]
        lam_prod = work[:, 2560:2560 + 128]

        A_G, KV_G, B_G, FFN_G, N1_G, N2_G, C_IN, BQ_G, LAT_G = 0, 8, 16, 24, 40, 72, 104, 112, 118
        MOD_B = P
        MOD = {0: 0, "kv": 48, 1: 64}
        SH1, SC1, G1, SH2, SC2, G2 = (k * KD for k in range(6))

        pairs = [ctx.enter_context(nc.psum_tensor(f"pair{i}", [P, 1024], F32)) for i in range(2)]
        Y = ctx.enter_context(nc.psum_tensor("Y", [P, 2048], F32))
        y_sum = Y[:, :].rearrange("p (b n) -> p b n", b=TB)
        pT_ps = Y[:, 0:1024].rearrange("p (h t) -> p h t", h=4)
        o_ps = [Y[:, 1024:1536], Y[:, 1536:2048]]

        const_loaded = sem("const_loaded")
        x_loaded = sem("x_loaded")
        slot_loaded = [sem(f"slot_loaded{i}") for i in range(RING)]
        chunk_done = sem("chunk_done")
        fill_done = sem("fill_done")
        emptied = [sem(f"emptied{i}") for i in range(2)]
        lam_ready = sem("lam_ready")
        half_ready = sem("half_ready")
        c_ready = sem("c_ready")
        updated = sem("updated")
        squared = sem("squared")
        mean_ready = sem("mean_ready")
        rs_ready = sem("rs_ready")
        scaled = sem("scaled")
        logf_ready = sem("logf_ready")
        turns_ready = sem("turns_ready")
        rope_ready = sem("rope_ready")
        softplus_ready = sem("softplus_ready")
        combined = sem("combined")
        gated_ready = sem("gated_ready")
        qk_ready = sem("qk_ready")
        max_ready = sem("max_ready")
        probs_ready = sem("probs_ready")
        pT_done = sem("pT_done")
        pT_ready = sem("pT_ready")
        pv_done = sem("pv_done")
        o_taken = sem("o_taken")
        o_ready = sem("o_ready")
        latent_ready = sem("latent_ready")
        r_pv_done = sem("r_pv_done")
        r_taken = sem("r_taken")
        rel_stored = sem("rel_stored")
        rel_loaded = sem("rel_loaded")
        gain_loaded = sem("gain_loaded")
        vchain = sem("vchain")
        achain = sem("achain")
        stored = sem("stored")

        def pair(use):
            return pairs[use.u % 2]

        def wait_full(eng, use, more_chunks=0):
            if use.chunk is not None:
                eng.wait_ge(chunk_done, more_chunks + (use.chunk + 1))
            else:
                eng.wait_ge(fill_done, use.fill + 1)

        def wait_emptied(eng, use, more_uses=0):
            eng.wait_ge(emptied[use.u % 2], more_uses + (use.u // 2 + 1))

        def wait_free(eng, use, more_uses=0):
            if use.u >= 2:
                eng.wait_ge(emptied[use.u % 2], more_uses + use.u // 2)

        def quads(ap):
            return ap.rearrange("p (f t) -> p f t", f=4)

        def tokpair(ap):
            return ap.rearrange("p (b n) -> p b n", b=TB)

        def row_blocks(name, r0, c0, at=None):
            v = w[name]
            v = v.rearrange("l (r c) -> (l r) c", c=P) if len(v.shape) == 2 else v.rearrange("(r c) -> r c", c=P)
            return rows[r0:r0 + v.shape[0], c0:c0 + P], v

        small_loads = [
            (squares[:], table["squares"]),
            row_blocks("a_norm_g", A_G, 0), row_blocks("kv_norm_g", KV_G, 0), row_blocks("b_norm_g", B_G, 0),
            row_blocks("ffn_norm_g", FFN_G, 0), row_blocks("norm1_2", N1_G, 0), row_blocks("norm2_2", N2_G, 0),
            row_blocks("c", C_IN, 0), row_blocks("b_q_norm_g", BQ_G, 0), row_blocks("kv_latent_g", LAT_G, 0),
            (rows[120:P, 0:P], table["squares"][0:P - 120, 0:P]),
            (rows[0:48, P:2 * P], w["b_mod"][0].rearrange("(r c) -> r c", c=P)),
            row_blocks("kv_b_mod", 48, P),
            (rows[64:112, P:2 * P], w["b_mod"][1].rearrange("(r c) -> r c", c=P)),
            (rows[112:P, P:2 * P], table["squares"][0:P - 112, 0:P]),
            (rel_in, w["rel_bias_2"]), (onehot, table["onehot"]),
            (lam_in, w["diff_lambda_2"].rearrange("l i d -> l (i d)").to_broadcast([P, 256])),
            (pos_i[:], w["positions"].rearrange("o (b p) -> p (o b)", p=P)),
            (small[:], table["small"]), (masks[:], table["masks"]),
            (w_f[:], w["a_w_in"][0].rearrange("(k p) n -> p k n", p=P)[:, :, 3 * D:3 * D + HEADS]),
            (b_f[:], w["a_b_f"].to_broadcast([P, HEADS])),
            (w_router[:], w["router_w"].rearrange("(k p) n -> p k n", p=P)),
            (r_bias[:], w["router_bias"].unsqueeze(0).to_broadcast([P, EXPERTS])),
            (decay[:].rearrange("p h t -> p (h t)"), table["decay"]),
            (rotary[:].rearrange("p i t -> p (i t)"), table["rotary"]),
            (subln[:], w["diff_subln_2"].rearrange("l (d o) -> d (l o)", o=1)),
        ] + [(head_gain[0:HD, i:i + 1], w[name].rearrange("l (d o) -> d (l o)", o=1)) for i, name in enumerate(
            ("moba_q_norm_2", "moba_k_norm_2", "diff_q_norm_2", "diff_k_norm_2"))]
        N_CONST = len(small_loads)

        block = ctx.enter_context(nc.Block())

        @block.sync
        def _(sp):
            def source(what):
                kind = what[0]
                if kind == "cols":
                    _, name, at, j = what
                    m = w[name]
                    if isinstance(at, tuple):
                        m = m[at[0], at[1]]
                    elif at is not None:
                        m = m[at]
                    return m.rearrange("(k p) n -> p k n", p=P)[:, :, j * 512:(j + 1) * 512]
                if kind == "rows":
                    _, (name, at), j = what
                    return w[name][at, j * 512:(j + 1) * 512, :].rearrange("(k p) n -> p k n", p=P)
                if kind == "rows_e":
                    _, name, (layer, e) = what
                    return w[name][layer, e].rearrange("(k p) n -> p k n", p=P)
                if kind == "kv_down":
                    return w["kv_w_down"].rearrange("(k p) n -> p k n", p=P)
                if kind == "kv_up":
                    return w["kv_w_up"].rearrange("(k p) n -> p k n", p=P)[:, :, what[1] * 512:(what[1] + 1) * 512]
                if kind == "dq_tail":
                    return w["b_w_dq"][0].rearrange("(k p) n -> p k n", p=P)[:, :, 512:768]
                if kind == "uq":
                    return w["b_w_uq"][0].rearrange("(k p) n -> p k n", p=P)[:, :, what[1] * 512:(what[1] + 1) * 512]

            def load(c, src, turns=0):
                if c >= RING:
                    sp.wait_ge(chunk_done, turns * RING + (c - RING + 1))
                k, n = src.shape[1], src.shape[2]
                dst = ring[:, c % RING, 0:k * n].rearrange("p (k n) -> p k n", k=k)
                sp.dma_start(dst, src).then_inc(slot_loaded[c % RING], 16)

            def load_range(a, b):
                for c in range(a, b):
                    load(c, source(plan.streamed[c]))

            def load_experts(m, layer, peeled, step):
                a, b = m.gate[peeled].chunk, m.gate[peeled + step].chunk
                turns = (EXPERTS - peeled) // step
                with sp.Fori(0, turns) as t:
                    slots = t * ((b - a) // RING)
                    for i in range(step):
                        e = t * step + (peeled + i)
                        load(m.gate[peeled + i].chunk,
                             w["exp_w_gate"][layer, bass.ds(e, 1)].rearrange("e (k p) n -> p (e k) n", p=P), slots)
                        load(m.up[peeled + i].chunk,
                             w["exp_w_up"][layer, bass.ds(e, 1)].rearrange("e (k p) n -> p (e k) n", p=P), slots)
                        load(m.down[peeled + i - 1],
                             w["exp_w_down"][layer, bass.ds(t * step + (peeled + i - 1), 1)]
                             .rearrange("e (k p) n -> p (e k) n", p=P), slots)
                        if m.mod:
                            j = t * (step * 512) + (peeled + i - 4) * 512
                            load(m.mod[peeled + i].chunk,
                                 w["w_mod"][1].rearrange("(k p) n -> p k n", p=P)[:, :, bass.ds(j, 512)], slots)
                return b + (b - a) * (turns - 1)

            def load_mlp(m, layer):
                a, b = m.up[2].chunk, m.up[4].chunk
                up = w["w_up_2"][layer].rearrange("(k p) n -> p k n", p=P)
                down = w["w_down_2"][layer].rearrange("(j k p) n -> j p k n", p=P, k=4)
                with sp.Fori(0, (FF_PARTS - 2) // 2) as t:
                    for i in range(2):
                        load(m.up[2 + i].chunk, up[:, :, bass.ds(t * 1024 + (2 + i) * 512, 512)], t)
                        load(m.down[1 + i], down[bass.ds(t * 2 + (1 + i), 1)].rearrange("j p k n -> p (j k) n"), t)
                return b + (b - a) * 2

            at = plan.moe0.gate[4].chunk
            load_range(0, at)
            at = load_experts(plan.moe0, 0, 4, 2)
            load_range(at, plan.moe1.gate[4].chunk)
            at = load_experts(plan.moe1, 1, 4, 4)
            for m, layer in ((plan.mlp0, 0), (plan.mlp1, 1), (plan.mlp2, 2), (plan.mlp3, 3)):
                load_range(at, m.up[2].chunk)
                at = load_mlp(m, layer)
            load_range(at, len(plan.streamed))
            for b in range(TB):
                sp.wait_ge(updated, TB * plan.mlp3.update + b + 1)
                sp.dma_start(out[0, b * P:(b + 1) * P, :], x[:, b, :]).then_inc(stored, 16)
            sp.wait_ge(stored, 16 * TB)

        @block.gpsimd
        def _(pool):
            nc.gpsimd.memset(minus_half[:], -0.5).then_inc(half_ready, 1)
            pool.wait_ge(half_ready, 1)
            for r, (n, inv) in enumerate(plan.stats):
                pool.wait_ge(squared, r + 1)
                v = ss[:, r % 2, 0:n]
                nc.gpsimd.tensor_scalar(v, v, inv, EPS, ALU.mult, ALU.add).then_inc(mean_ready, 1)
                pool.wait_ge(mean_ready, r + 1)
                nc.gpsimd.tensor_tensor(rs[:, r % 2, 0:n], v, minus_half[:, 0:n], ALU.pow).then_inc(rs_ready, 1)

        @block.tensor
        def _(pe):
            def slot(c, k, n):
                return ring[:, c % RING, 0:k * n].rearrange("p (k n) -> p k n", k=k)

            def wait_loaded(c, turns=0):
                pe.wait_ge(slot_loaded[c % RING], turns * 16 + 16 * (c // RING + 1))

            def transposed_product(use, turns=0, more_uses=0):
                wt, ps = slot(use.chunk, KD, 512), quads(pair(use)[:, :])
                wait_loaded(use.chunk, turns)
                wait_free(pe, use, more_uses)
                for f in range(4):
                    for k in range(KD):
                        last = nc.tensor.matmul(ps[:, f, :], wt[:, k, f * P:(f + 1) * P], hT[:, k, :],
                                                start=(k == 0), stop=(k == KD - 1))
                last.then_inc(chunk_done, 1)

            def token_product(use, lhs, k_blocks=KD, n=512):
                wt, ps = slot(use.chunk, k_blocks, n), tokpair(pair(use)[:, :])
                wait_loaded(use.chunk)
                wait_free(pe, use)
                for b in range(TB):
                    for k in range(k_blocks):
                        last = nc.tensor.matmul(ps[:, b, 0:n], lhs[:, k, b * P:(b + 1) * P], wt[:, k, :],
                                                start=(k == 0), stop=(k == k_blocks - 1))
                last.then_inc(chunk_done, 1)

            def modulation(use, turns=0, more_uses=0):
                wt, ps = slot(use.chunk, KD, 512), pair(use)
                wait_loaded(use.chunk, turns)
                wait_free(pe, use, more_uses)
                for f in range(4):
                    for k in range(KD):
                        last = nc.tensor.matmul(ps[:, f:f + 1], wt[:, k, f * P:(f + 1) * P], c_act[:, k:k + 1],
                                                start=(k == 0), stop=(k == KD - 1))
                last.then_inc(chunk_done, 1)

            def down_product(c, lhs, first, last_one, turns=0):
                wt = slot(c, 4, D)
                wait_loaded(c, turns)
                for b in range(TB):
                    for n in range(2):
                        for k in range(4):
                            last = nc.tensor.matmul(y_sum[:, b, n * 512:(n + 1) * 512],
                                                    lhs[:, k, b * P:(b + 1) * P],
                                                    wt[:, k, n * 512:(n + 1) * 512],
                                                    start=(first and k == 0), stop=(last_one and k == 3))
                last.then_inc(chunk_done, 1)

            def transposes(use, src, k0, n=4):
                ps = quads(pair(use)[:, :])
                wait_free(pe, use)
                for b in range(TB):
                    for k in range(n):
                        last = nc.tensor.transpose(ps[:, k, b * P:(b + 1) * P],
                                                   src[:, b, (k0 + k) * P:(k0 + k + 1) * P], ident)
                last.then_inc(fill_done, 1)

            def norm(n):
                pe.wait_ge(scaled, TB * (n.scaled + 1))
                for j in range(2):
                    transposes(n.uses[j], xn, 4 * j)
                wait_emptied(pe, n.uses[1])

            def gate_rows(uses, layer):
                for use, at in zip(uses, (G1, G2)):
                    wait_free(pe, use)
                    for k in range(KD):
                        j = MOD[layer] + at + k
                        last = nc.tensor.matmul(pair(use)[:, k * P:(k + 1) * P],
                                                mod[:, j:j + 1].to_broadcast([P, P]), ident, start=True, stop=True)
                    last.then_inc(fill_done, 1)

            def attention(a, dh, q_tok, k_tok, dv, o_wait):
                for g in range(4):
                    for use, src in zip(a.kq[2 * g:2 * g + 2], (q_tok, k_tok)):
                        wait_free(pe, use)
                        ps = quads(pair(use)[:, :])
                        for i in range(4):
                            for b in range(TB):
                                h = 4 * g + i
                                last = nc.tensor.transpose(ps[0:dh, i, b * P:(b + 1) * P],
                                                           src[:, b, h * dh:(h + 1) * dh], ident)
                        last.then_inc(fill_done, 1)
                for use in a.kq[-2:]:
                    wait_emptied(pe, use)

                def scores(n):
                    g, qb = n // 2, n % 2
                    use = a.scores[n]
                    ps = quads(pair(use)[:, :])
                    wait_free(pe, use)
                    for i in range(4):
                        h = 4 * g + i
                        last = nc.tensor.matmul(ps[:, i, 0:(qb + 1) * P], qT[0:dh, h, qb * P:(qb + 1) * P],
                                                kT[0:dh, h, 0:(qb + 1) * P], start=True, stop=True)
                    last.then_inc(fill_done, 1)

                def weigh(n):
                    g, qb, at = n // 2, n % 2, a.unit + n
                    pe.wait_ge(probs_ready, at + 1)
                    if at >= 1:
                        pe.wait_ge(pT_ready, at)
                    for i in range(4):
                        for kb in range(qb + 1):
                            last = nc.tensor.transpose(pT_ps[:, i, kb * P:(kb + 1) * P],
                                                       probs[:, n % 2, i, kb * P:(kb + 1) * P], ident)
                    last.then_inc(pT_done, 1)
                    pe.wait_ge(pT_ready, at + 1)
                    if at >= 2:
                        pe.wait_ge(o_taken, at - 1)
                    for i in range(4):
                        h = 4 * g + i
                        v0 = (h * HD) if dv == HD else (h // 2) * dv
                        for kb in range(qb + 1):
                            last = nc.tensor.matmul(o_ps[n % 2][:, i * dv:(i + 1) * dv],
                                                    pT[:, n % 2, i, kb * P:(kb + 1) * P],
                                                    v_tok[:, kb, v0:v0 + dv], start=(kb == 0), stop=(kb == qb))
                    last.then_inc(pv_done, 1)

                scores(0)
                for n in range(8):
                    if n < 7:
                        scores(n + 1)
                    weigh(n)
                o_wait()
                for j in range(2):
                    transposes(a.oT[j], o_tok, 4 * j)
                wait_emptied(pe, a.oT[1])
                for j in range(2):
                    down_product(a.wo[j], hT[:, 4 * j:4 * j + 4, :], j == 0, j == 1)

            def attention_done(a):
                def wait():
                    pe.wait_ge(o_taken, a.unit + 8)
                return wait

            def experts(m, peeled, step):
                norm(m.norm)
                use = m.router
                wait_free(pe, use)
                for b in range(TB):
                    for k in range(KD):
                        last = nc.tensor.matmul(pair(use)[:, b * EXPERTS:(b + 1) * EXPERTS],
                                                hT[:, k, b * P:(b + 1) * P], w_router[:, k, :],
                                                start=(k == 0), stop=(k == KD - 1))
                last.then_inc(fill_done, 1)

                def down(e, slots=0, more=0):
                    pe.wait_ge(gated_ready, more + (m.first + e + 1))
                    down_product(m.down[e], gated[:, (m.first + e) % 2], e == 0, e == EXPERTS - 1, slots)

                def one(e, slots=0, uses=0, more=0):
                    transposed_product(m.gate[e], slots, uses)
                    transposed_product(m.up[e], slots, uses)
                    if e:
                        down(e - 1, slots, more)
                    if m.mod:
                        modulation(m.mod[e], slots, uses)

                for e in range(peeled):
                    one(e)
                    if e == 0:
                        pe.wait_ge(combined, (1 if m is plan.moe0 else 2))
                        for j, use in enumerate(m.comb):
                            wait_free(pe, use)
                            ps = quads(pair(use)[:, :])
                            for i in range(4):
                                for b in range(TB):
                                    col = route[:, 9, b * EXPERTS + 4 * j + i:b * EXPERTS + 4 * j + i + 1]
                                    last = nc.tensor.matmul(ps[:, i, b * P:(b + 1) * P],
                                                            col.to_broadcast([P, P]), ident, start=True, stop=True)
                            last.then_inc(fill_done, 1)
                chunks = m.gate[peeled + step].chunk - m.gate[peeled].chunk
                uses = m.gate[peeled + step].u - m.gate[peeled].u
                with pe.Fori(0, (EXPERTS - peeled) // step) as t:
                    for i in range(step):
                        one(peeled + i, t * (chunks // RING), t * (uses // 2), t * step)
                down(EXPERTS - 1)

            def mlp(m):
                norm(m.norm)

                def down(j, slots=0, more=0):
                    pe.wait_ge(gated_ready, more + (m.first + j + 1))
                    down_product(m.down[j], gated[:, (m.first + j) % 2], j == 0, j == FF_PARTS - 1, slots)

                transposed_product(m.up[0])
                transposed_product(m.up[1])
                down(0)
                with pe.Fori(0, (FF_PARTS - 2) // 2) as t:
                    for i in range(2):
                        transposed_product(m.up[2 + i], t, t)
                        down(1 + i, t, t * 2)
                down(FF_PARTS - 1)

            def retention(r):
                norm(r.norm)
                for c, use in enumerate(r.proj):
                    if c < 4:
                        transposed_product(use)
                    else:
                        token_product(use, hT)
                wait_emptied(pe, r.proj[3])
                wait_emptied(pe, r.proj[7])

                def scores(h):
                    use = r.scores[h]
                    ps = pair(use)
                    wait_free(pe, use)
                    for half in range(2):
                        nc.tensor.matmul(ps[:, 0:S], r_kT[:, 2 * h + half, 0:P], r_qT[:, 2 * h + half, :],
                                         start=(half == 0), stop=(half == 1))
                    for half in range(2):
                        last = nc.tensor.matmul(ps[:, 512:512 + P], r_kT[:, 2 * h + half, P:S],
                                                r_qT[:, 2 * h + half, P:S], start=(half == 0), stop=(half == 1))
                    last.then_inc(fill_done, 1)

                def weigh(h):
                    wait_emptied(pe, r.scores[h])
                    if r.head + h >= 2:
                        pe.wait_ge(r_taken, r.head + h - 1)
                    o = tokpair(Y[:, (h % 2) * 1024:(h % 2 + 1) * 1024])
                    sT, vs = r_s[:, h % 2], slice(h * RDV, (h + 1) * RDV)
                    nc.tensor.matmul(o[:, 0, :], sT[:, 0:P], r_v[:, 0, vs], start=True, stop=True)
                    nc.tensor.matmul(o[:, 1, :], sT[:, P:S], r_v[:, 0, vs], start=True, stop=False)
                    nc.tensor.matmul(o[:, 1, :], sT[:, S:S + P], r_v[:, 1, vs],
                                     start=False, stop=True).then_inc(r_pv_done, 1)

                scores(0)
                for h in range(RH):
                    if h + 1 < RH:
                        scores(h + 1)
                    weigh(h)
                pe.wait_ge(r_taken, r.head + RH)
                for j in range(4):
                    transposes(r.oT[j], r_o, 4 * j)
                for j in range(4):
                    wait_emptied(pe, r.oT[j])
                    down_product(r.wo[j], r_oT[:, 4 * j:4 * j + 4, :], j == 0, j == 3)

            pe.wait_ge(const_loaded, 16 * N_CONST)
            use = plan.columns
            nc.tensor.transpose(pair(use)[:, 0:P], rows[:, 0:P], ident)
            nc.tensor.transpose(pair(use)[:, P:2 * P], rows[:, P:2 * P], ident).then_inc(fill_done, 1)
            nc.tensor.matmul(pair(plan.rel)[0:16, 0:S], rel_in, onehot, start=True, stop=True).then_inc(fill_done, 1)
            pe.wait_ge(c_ready, 1)
            for use in plan.mod_a:
                modulation(use)
            norm(plan.a_norm)
            use = plan.f_logit
            wait_free(pe, use)
            for b in range(TB):
                for k in range(KD):
                    last = nc.tensor.matmul(pair(use)[:, b * HEADS:(b + 1) * HEADS], hT[:, k, b * P:(b + 1) * P],
                                            w_f[:, k, :], start=(k == 0), stop=(k == KD - 1))
            last.then_inc(fill_done, 1)
            for j in range(6):
                token_product(plan.a_proj[j], hT)
                for use in plan.a_mods[j]:
                    modulation(use)
                if j == 0:
                    pe.wait_ge(logf_ready, 1)
                    use = plan.cum_q
                    wait_free(pe, use)
                    nc.tensor.matmul(pair(use)[:, 0:HEADS], upto_m, logf[:, 0, :], start=True, stop=True)
                    nc.tensor.matmul(pair(use)[:, HEADS:2 * HEADS], ones_m, logf[:, 0, :], start=True, stop=False)
                    nc.tensor.matmul(pair(use)[:, HEADS:2 * HEADS], upto_m, logf[:, 1, :],
                                     start=False, stop=True).then_inc(fill_done, 1)
                    for g, use in enumerate(plan.cum_k):
                        wait_free(pe, use)
                        ps = quads(pair(use)[:, :])
                        for i in range(4):
                            h = 4 * g + i
                            f0 = logf[:, 0, h:h + 1].to_broadcast([P, P])
                            f1 = logf[:, 1, h:h + 1].to_broadcast([P, P])
                            nc.tensor.matmul(ps[:, i, 0:P], f0, upto_m, start=True, stop=True)
                            nc.tensor.matmul(ps[:, i, P:S], f0, ones_m, start=True, stop=False)
                            last = nc.tensor.matmul(ps[:, i, P:S], f1, upto_m, start=False, stop=True)
                        last.then_inc(fill_done, 1)
            wait_emptied(pe, plan.a_mods[5][-1])
            gate_rows(plan.gates_a, 0)
            wait_emptied(pe, plan.a_proj[5])
            attention(plan.att_a, HD, tokpair(q_area[:, 0:2048]), tokpair(k_area[:, 0:2048]), HD,
                      attention_done(plan.att_a))
            experts(plan.moe0, 4, 2)
            norm(plan.kv_norm)
            token_product(plan.kv_down, hT, KD, KV_RANK + ROPE)
            pe.wait_ge(latent_ready, 1)
            use = plan.ckvT
            wait_free(pe, use)
            for b in range(TB):
                for k in range(2):
                    last = nc.tensor.transpose(quads(pair(use)[:, :])[:, k, b * P:(b + 1) * P],
                                               ckv[:, b, k * P:(k + 1) * P], ident)
            last.then_inc(fill_done, 1)
            wait_emptied(pe, use)
            for use in plan.kv_up:
                token_product(use, ckvT, 2)
            norm(plan.b_norm)
            token_product(plan.dq[0], hT)
            token_product(plan.dq[1], hT, KD, 256)
            pe.wait_ge(latent_ready, 2)
            transposes(plan.cqT[0], cq, 0)
            transposes(plan.cqT[1], cq, 4, 2)
            wait_emptied(pe, plan.cqT[1])
            for use in plan.uq:
                token_product(use, cqT, 6)
            gate_rows(plan.gates_b, 1)
            pe.wait_ge(qk_ready, 1)
            attention(plan.att_b, QK_B, tokpair(q_area), tokpair(k_area), HD, attention_done(plan.att_b))
            experts(plan.moe1, 4, 4)
            retention(plan.ret0)
            mlp(plan.mlp0)

            def softmax_layer(a, nth, mlp_plan_):
                norm(a.norm)
                for use in a.proj:
                    token_product(use, hT)
                pe.wait_ge(qk_ready, nth)
                wait_emptied(pe, a.proj[5])
                if a.diff:
                    def o_wait():
                        pe.wait_ge(o_ready, 1)
                    dv = 2 * HD
                else:
                    o_wait, dv = attention_done(a.att), HD
                attention(a.att, HD, tokpair(q_area[:, 0:2048]), tokpair(k_area[:, 0:2048]), dv, o_wait)
                mlp(mlp_plan_)

            softmax_layer(plan.moba, 2, plan.mlp1)
            softmax_layer(plan.diff, 3, plan.mlp2)
            retention(plan.ret1)
            mlp(plan.mlp3)

        @block.scalar
        def _(se):
            links = [0]

            def link(ins):
                links[0] += 1
                ins.then_inc(achain, 1)
                se.wait_ge(achain, links[0])

            def squares_of(src, stat, waits, scratch=0):
                for b in range(TB):
                    waits(b)
                    n = src[b].shape[1]
                    last = nc.scalar.activation(xn[:, b, scratch:scratch + n], src[b], ACT.Square,
                                                accum_out=ss[:, stat % 2, b:b + 1])
                last.then_inc(squared, 1)

            def norm(n):
                def waits(b):
                    if n.after:
                        se.wait_ge(updated, TB * (n.after - 1) + b + 1)
                    else:
                        se.wait_ge(x_loaded, 16)
                squares_of([x[:, b, :] for b in range(TB)], n.stat, waits)

            def copy_out(dst, use, src):
                wait_full(se, use)
                nc.scalar.activation(dst, src, ACT.Copy).then_inc(emptied[use.u % 2], 1)

            def attention(a, dh, q_scale):
                for g in range(4):
                    use = a.kq[2 * g]
                    copy = ACT.Copy if q_scale is None else ACT.Identity
                    more = {} if q_scale is None else {"scale": q_scale}
                    wait_full(se, use)
                    nc.scalar.activation(qT[0:dh, 4 * g:4 * g + 4, :], quads(pair(use)[:, :])[0:dh], copy,
                                         **more).then_inc(emptied[use.u % 2], 1)

                def exponentials(n):
                    nk = (n % 2 + 1) * P
                    se.wait_ge(max_ready, a.unit + n + 1)
                    for i in range(4):
                        p = probs[:, n % 2, i, 0:nk]
                        last = nc.scalar.activation(p, p, ACT.Exp, bias=negmax[:, n % 2, i:i + 1],
                                                    accum_out=expsum[:, n % 2, i:i + 1])
                    last.then_inc(probs_ready, 1)

                exponentials(0)
                for n in range(8):
                    if n < 7:
                        exponentials(n + 1)
                    nk = (n % 2 + 1) * P
                    se.wait_ge(pT_done, a.unit + n + 1)
                    nc.scalar.activation(pT[:, n % 2, :, 0:nk], pT_ps[:, :, 0:nk], ACT.Copy).then_inc(pT_ready, 1)

            def experts(m, peeled, step):
                norm(m.norm)
                wait_full(se, m.router)
                nc.scalar.activation(route[:, 0, :], pair(m.router)[:, 0:TB * EXPERTS],
                                     ACT.Sigmoid).then_inc(emptied[m.router.u % 2], 1)

                def one(e, chunks=0):
                    use = m.gate[e]
                    wait_full(se, use, chunks)
                    nc.scalar.activation(act[:, (m.first + e) % 2], quads(pair(use)[:, :]),
                                         ACT.Silu).then_inc(emptied[use.u % 2], 1)

                one(0)
                for j, use in enumerate(m.comb):
                    copy_out(comb[:, 4 * j:4 * j + 4, :], use, quads(pair(use)[:, :]))
                for e in range(1, peeled):
                    one(e)
                chunks = m.gate[peeled + step].chunk - m.gate[peeled].chunk
                with se.Fori(0, (EXPERTS - peeled) // step) as t:
                    for i in range(step):
                        one(peeled + i, t * chunks)

            def mlp(m):
                norm(m.norm)

                def one(j, chunks=0):
                    use = m.up[j]
                    wait_full(se, use, chunks)
                    nc.scalar.activation(act[:, (m.first + j) % 2], quads(pair(use)[:, :]),
                                         ACT.Relu).then_inc(emptied[use.u % 2], 1)
                one(0)
                one(1)
                with se.Fori(0, (FF_PARTS - 2) // 2) as t:
                    for i in range(2):
                        one(2 + i, t * 4)

            def retention(r):
                norm(r.norm)
                for c in range(4):
                    use = r.proj[4 + c]
                    copy_out(r_v[:, :, c * 512:(c + 1) * 512], use, tokpair(pair(use)[:, :]))
                for c in range(4):
                    use = r.proj[8 + c]
                    wait_full(se, use)
                    nc.scalar.activation(r_g[:, :, c * 512:(c + 1) * 512], tokpair(pair(use)[:, :]),
                                         ACT.Silu).then_inc(emptied[use.u % 2], 1)
                for h in range(RH):
                    se.wait_ge(r_pv_done, r.head + h + 1)
                    o = tokpair(Y[:, (h % 2) * 1024:(h % 2 + 1) * 1024])
                    squares_of([o[:, b, :] for b in range(TB)], r.stat[h], lambda b: None, (h % 2) * RDV)
                for j in (1, 3):
                    use = r.oT[j]
                    copy_out(r_oT[:, 4 * j:4 * j + 4, :], use, quads(pair(use)[:, :]))

            for dst, src in small_loads:
                se.dma_start(dst, src, allow_slow_non_contiguous=True).then_inc(const_loaded, 16)
            se.dma_start(x[:], w["x"][0].rearrange("(b p) n -> p b n", p=P)).then_inc(x_loaded, 16)
            wait_full(se, plan.rel)
            wait_emptied(se, plan.columns)
            nc.scalar.activation(c_act[:], cols[:, C_IN:C_IN + KD], ACT.Silu).then_inc(c_ready, 1)
            wait_emptied(se, plan.rel)
            se.dma_start(rel_scratch, spread(rel_rows, 1, P)).then_inc(rel_stored, 16)
            se.wait_ge(lam_ready, 1)
            nc.scalar.activation(lam[:, 2:4], lam[:, 0:2], ACT.Exp).then_inc(lam_ready, 1)
            se.wait_ge(turns_ready, 1)
            nc.scalar.activation(rope[:], ropew[:], ACT.Sin).then_inc(rope_ready, 1)
            norm(plan.a_norm)
            se.wait_ge(rel_stored, 16)
            wait_emptied(se, plan.f_logit)
            link(nc.scalar.activation(logw[:], cumq[:], ACT.Abs))
            link(nc.scalar.activation(logw[:], logw[:], ACT.Exp, scale=-1.0))
            nc.scalar.activation(logw[:], logw[:], ACT.Ln, bias=1.0).then_inc(softplus_ready, 1)
            for j in range(6):
                use, half = plan.a_proj[j], (j % 2) * 512
                area = (q_area[:, 0:2048], k_area[:, 0:2048], work[:, 6144:8192])[j // 2]
                copy_out(tokpair(area)[:, :, half:half + 512], use, tokpair(pair(use)[:, :]))
            for i, use in enumerate(plan.gates_a):
                copy_out(gates[:, i, :], use, pair(use)[:, :])
            attention(plan.att_a, HD, None)
            experts(plan.moe0, 4, 2)
            norm(plan.kv_norm)
            use = plan.kv_down
            copy_out(ckv, use, tokpair(pair(use)[:, :])[:, :, 0:KV_RANK + ROPE])
            wait_emptied(se, use)
            squares_of([ckv[:, b, 0:KV_RANK] for b in range(TB)], plan.kv_stat, lambda b: None)
            for j, use in enumerate(plan.kv_up):
                wait_full(se, use)
                ps = pair(use)[:, :].rearrange("p (b h n) -> p b h n", b=TB, h=4)
                kv = tokpair(k_area).rearrange("p b (h n) -> p b h n", h=HEADS)[:, :, 4 * j:4 * j + 4, 0:NOPE]
                vv = v_tok.rearrange("p b (h n) -> p b h n", h=HEADS)[:, :, 4 * j:4 * j + 4, :]
                for b in range(TB):
                    nc.scalar.activation(kv[:, b], ps[:, b, :, 0:NOPE], ACT.Copy)
                    last = nc.scalar.activation(vv[:, b], ps[:, b, :, NOPE:2 * NOPE], ACT.Copy)
                last.then_inc(emptied[use.u % 2], 1)
            norm(plan.b_norm)
            copy_out(cq[:, :, 0:512], plan.dq[0], tokpair(pair(plan.dq[0])[:, :]))
            copy_out(cq[:, :, 512:768], plan.dq[1], tokpair(pair(plan.dq[1])[:, :])[:, :, 0:256])
            wait_emptied(se, plan.dq[0])
            wait_emptied(se, plan.dq[1])
            squares_of([cq[:, b, :] for b in range(TB)], plan.cq_stat, lambda b: None)
            for j, use in enumerate(plan.uq):
                copy_out(tokpair(q_area)[:, :, j * 512:(j + 1) * 512], use, tokpair(pair(use)[:, :]))
            for i, use in enumerate(plan.gates_b):
                copy_out(gates[:, i, :], use, pair(use)[:, :])
            attention(plan.att_b, QK_B, None)
            se.wait_ge(updated, TB * (plan.att_b.update + 1))
            se.dma_start(gates[:, 0, :], w["final_norm_g"].unsqueeze(0).to_broadcast([P, D])).then_inc(gain_loaded, 16)
            experts(plan.moe1, 4, 4)
            squares_of([x[:, b, :] for b in range(TB)], plan.final_stat,
                       lambda b: se.wait_ge(updated, TB * plan.moe1.update + b + 1))
            retention(plan.ret0)
            se.wait_ge(chunk_done, plan.ret0.wo[3] + 1)
            se.wait_ge(rel_stored, 16)
            rows_at = bass.AP(rel_scratch.tensor, P - 1, [[383, P], [384 * P, HEADS], [1, S]])
            se.dma_start(relbias, rows_at).then_inc(rel_loaded, 16)
            mlp(plan.mlp0)

            def softmax_layer(a, nth):
                norm(a.norm)
                for j in range(6):
                    use, half = a.proj[j], (j % 2) * 512
                    area = (q_area[:, 0:2048], k_area[:, 0:2048], work[:, 6144:8192])[j // 2]
                    copy_out(tokpair(area)[:, :, half:half + 512], use, tokpair(pair(use)[:, :]))
                attention(a.att, HD, head_gain[0:HD, 2 * nth:2 * nth + 1])

            softmax_layer(plan.moba, 0)
            mlp(plan.mlp1)
            softmax_layer(plan.diff, 1)
            mlp(plan.mlp2)
            retention(plan.ret1)
            mlp(plan.mlp3)

        @block.vector
        def _(ve):
            links = [0]
            V = nc.vector

            def link(ins):
                links[0] += 1
                ins.then_inc(vchain, 1)
                ve.wait_ge(vchain, links[0])

            def empties(use, ins):
                ins.then_inc(emptied[use.u % 2], 1)

            def modulation(use, j):
                wait_full(ve, use)
                empties(use, V.tensor_tensor(mod[:, j:j + 4], pair(use)[:, 0:4], cols[:, MOD_B + j:MOD_B + j + 4],
                                             ALU.add))

            def gain_of(g, scale):
                link(V.scalar_tensor_tensor(gain[:], mod[:, scale:scale + KD], 1.0, cols[:, g:g + KD],
                                            ALU.add, ALU.mult))

            def norm(n, g, shift=None):
                ve.wait_ge(rs_ready, n.stat + 1)
                for b in range(TB):
                    V.tensor_scalar(xn[:, b, :], x[:, b, :], rs[:, n.stat % 2, b:b + 1], None,
                                    ALU.mult).then_inc(scaled, 1)
                for j, use in enumerate(n.uses):
                    wait_full(ve, use)
                    ps = quads(pair(use)[:, :])
                    for i in range(4):
                        k = 4 * j + i
                        if shift is None:
                            last = V.tensor_scalar(hT[:, k, :], ps[:, i, :], g[:, k:k + 1], None, ALU.mult)
                        else:
                            last = V.tensor_scalar(hT[:, k, :], ps[:, i, :], g[:, k:k + 1],
                                                   mod[:, shift + k:shift + k + 1], ALU.mult, ALU.add)
                    empties(use, last)

            def update(m_update, last_chunk, gate=None):
                ve.wait_ge(chunk_done, last_chunk + 1)
                for b in range(TB):
                    if gate is None:
                        V.tensor_tensor(x[:, b, :], x[:, b, :], y_sum[:, b, :], ALU.add).then_inc(updated, 1)
                    else:
                        link(V.tensor_tensor(xn[:, b, :], gates[:, gate, :], y_sum[:, b, :], ALU.mult))
                        V.tensor_tensor(x[:, b, :], x[:, b, :], xn[:, b, :], ALU.add).then_inc(updated, 1)

            def attention(a, dh, scale, bias, k_scale=None, diff=False, subln_stat=None):
                for g in range(4):
                    use = a.kq[2 * g + 1]
                    wait_full(ve, use)
                    src = quads(pair(use)[:, :])[0:dh]
                    dst = kT[0:dh, 4 * g:4 * g + 4, :]
                    if k_scale is None:
                        empties(use, V.tensor_copy(dst, src))
                    else:
                        empties(use, V.tensor_scalar(dst, src, k_scale, None, ALU.mult))

                def start(n):
                    g, nk, use = n // 2, (n % 2 + 1) * P, a.scores[n]
                    wait_full(ve, use)
                    s = probs[:, n % 2, :, 0:nk]
                    empties(use, V.scalar_tensor_tensor(s, quads(pair(use)[:, :])[:, :, 0:nk], scale,
                                                        bias(g, n % 2), ALU.mult, ALU.add))
                    wait_emptied(ve, use)
                    V.tensor_reduce(negmax[:, n % 2, :], s, X, ALU.max, negate=True).then_inc(max_ready, 1)

                def finish(n):
                    g, qb = n // 2, n % 2
                    ve.wait_ge(pv_done, a.unit + n + 1)
                    link(V.reciprocal(recip[:, n % 2, :], expsum[:, n % 2, :]))
                    dv = 2 * HD if diff else HD
                    o = o_ps[n % 2][:, 0:4 * dv].rearrange("p (h d) -> p h d", h=4)
                    r = spread(recip[:, n % 2, :], 2, dv)
                    if not diff:
                        V.tensor_tensor(o_tok[:, qb, g * 256:(g + 1) * 256].rearrange("p (h d) -> p h d", h=4),
                                        o, r, ALU.mult).then_inc(o_taken, 1)
                        return
                    V.tensor_tensor(diff_tmp.rearrange("p j i d -> p (j i) d"), o, r, ALU.mult).then_inc(o_taken, 1)
                    ve.wait_ge(o_taken, a.unit + n + 1)
                    link(V.scalar_tensor_tensor(
                        o_tok[:, qb, g * 256:(g + 1) * 256].rearrange("p (j d) -> p j d", j=2),
                        diff_tmp[:, :, 1, :], lam[:, 5:6], diff_tmp[:, :, 0, :], ALU.mult, ALU.add))

                start(0)
                for n in range(8):
                    if n < 7:
                        start(n + 1)
                    finish(n)
                if diff:
                    sq = work[:, 0:2048]
                    link(V.tensor_tensor(sq, o_flat, o_flat, ALU.mult))
                    V.tensor_reduce(ss[:, subln_stat % 2, 0:16], sq.rearrange("p (h d) -> p h d", d=2 * HD), X,
                                    ALU.add).then_inc(squared, 1)
                    ve.wait_ge(rs_ready, subln_stat + 1)
                    oh = o_flat.rearrange("p (h d) -> p h d", d=2 * HD)
                    V.tensor_tensor(oh, oh, spread(rs[:, subln_stat % 2, 0:16], 2, 2 * HD), ALU.mult).then_inc(o_ready, 1)
                for j, use in enumerate(a.oT):
                    wait_full(ve, use)
                    src, dst = quads(pair(use)[:, :]), hT[:, 4 * j:4 * j + 4, :]
                    if diff:
                        empties(use, V.tensor_scalar(dst, src, subln[:, 0:1], 1.0 - LAMBDA_INIT, ALU.mult, ALU.mult))
                    else:
                        empties(use, V.tensor_copy(dst, src))

            def routing(nth):
                R = [route[:, k, :] for k in range(10)]
                sc, sel = R[0], R[1]
                G8 = TB * GROUPS

                def fours(ap):
                    return ap.rearrange("p (g e) -> p g e", e=4)

                link(V.tensor_tensor(sel.rearrange("p (b e) -> p b e", b=TB), sc.rearrange("p (b e) -> p b e", b=TB),
                                     spread(r_bias[:, :], 1, TB), ALU.add))
                s4 = sel.rearrange("p (g i j) -> p g i j", g=G8, i=2)
                hi, lo = R[2][:, 0:16], R[2][:, 16:32]
                hi2, lo2 = hi.rearrange("p (g i) -> p g i", i=2), lo.rearrange("p (g i) -> p g i", i=2)
                link(V.tensor_tensor(hi2, s4[:, :, :, 0], s4[:, :, :, 1], ALU.max))
                link(V.tensor_tensor(lo2, s4[:, :, :, 0], s4[:, :, :, 1], ALU.min))
                top1, mid, low, top2 = (R[3][:, 8 * k:8 * k + 8] for k in range(4))
                link(V.tensor_tensor(top1, hi2[:, :, 0], hi2[:, :, 1], ALU.max))
                link(V.tensor_tensor(mid, hi2[:, :, 0], hi2[:, :, 1], ALU.min))
                link(V.tensor_tensor(low, lo2[:, :, 0], lo2[:, :, 1], ALU.max))
                link(V.tensor_tensor(top2, mid, low, ALU.max))
                gs, best, mark = R[4][:, 0:8], R[4][:, 8:10], R[4][:, 16:24]
                first, here = R[4][:, 10:12], R[4][:, 24:32]

                def by_block(ap):
                    return ap.rearrange("p (b g) -> p b g", b=TB)

                link(V.tensor_tensor(gs, top1, top2, ALU.add))
                link(V.tensor_reduce(best, by_block(gs), X, ALU.max))
                link(V.tensor_tensor(by_block(mark), by_block(gs), spread(best, 2, GROUPS), ALU.is_ge))
                link(V.tensor_tensor(by_block(mark), by_block(mark), spread(descending, 1, TB), ALU.mult))
                link(V.tensor_reduce(first, by_block(mark), X, ALU.max))
                link(V.tensor_tensor(by_block(here), by_block(mark), spread(first, 2, GROUPS), ALU.is_equal))
                m1, m2 = R[5][:, 0:8], R[5][:, 8:16]
                link(V.tensor_tensor(fours(R[6]), fours(sel), spread(top1, 2, 4), ALU.is_ge))
                link(V.tensor_tensor(fours(R[6]), fours(R[6]), spread(descending, 1, G8), ALU.mult))
                link(V.tensor_reduce(m1, fours(R[6]), X, ALU.max))
                link(V.tensor_tensor(fours(R[6]), fours(R[6]), spread(m1, 2, 4), ALU.is_equal))
                link(V.scalar_tensor_tensor(R[7], R[6], NEG, sel, ALU.mult, ALU.add))
                link(V.tensor_reduce(m2, fours(R[7]), X, ALU.max))
                link(V.tensor_tensor(fours(R[8]), fours(R[7]), spread(m2, 2, 4), ALU.is_ge))
                link(V.tensor_tensor(fours(R[8]), fours(R[8]), spread(descending, 1, G8), ALU.mult))
                link(V.tensor_reduce(m1, fours(R[8]), X, ALU.max))
                link(V.tensor_tensor(fours(R[8]), fours(R[8]), spread(m1, 2, 4), ALU.is_equal))
                link(V.tensor_tensor(R[6], R[6], R[8], ALU.add))
                link(V.tensor_tensor(fours(R[6]), fours(R[6]), spread(here, 2, 4), ALU.mult))
                link(V.tensor_tensor(R[6], R[6], sc, ALU.mult))
                link(V.tensor_reduce(R[5][:, 16:18], R[6].rearrange("p (b e) -> p b e", b=TB), X, ALU.add))
                link(V.reciprocal(R[5][:, 18:20], R[5][:, 16:18]))
                V.tensor_tensor(R[9].rearrange("p (b e) -> p b e", b=TB), R[6].rearrange("p (b e) -> p b e", b=TB),
                                spread(R[5][:, 18:20], 2, EXPERTS), ALU.mult).then_inc(combined, 1)

            def experts(m, nth, layer, peeled, step):
                if m.mod:
                    wait_emptied(ve, plan.a_mods[5][-1])
                gain_of(FFN_G + layer * KD, MOD[layer] + SC2)
                norm(m.norm, gain, MOD[layer] + SH2)
                wait_emptied(ve, m.router)
                routing(nth)

                def one(e, t=None, chunks=0, uses=0):
                    up = m.up[e]
                    if m.first + e:
                        ve.wait_ge(gated_ready, (0 if t is None else t * step) + (m.first + e))
                    wait_emptied(ve, m.gate[e], uses)
                    wait_full(ve, up, chunks)
                    at = (m.first + e) % 2
                    empties(up, V.tensor_tensor(prod, act[:, at], quads(pair(up)[:, :]), ALU.mult))
                    wait_emptied(ve, up, uses)
                    if m.mod:
                        use, j = m.mod[e], MOD["kv"] + 4 * e
                        wait_full(ve, use, chunks)
                        if t is None:
                            dst, bias = mod[:, j:j + 4], cols[:, MOD_B + j:MOD_B + j + 4]
                        else:
                            dst = mod[:, bass.ds(t * (4 * step) + j, 4)]
                            bias = cols[:, bass.ds(t * (4 * step) + (MOD_B + j), 4)]
                        empties(use, V.tensor_tensor(dst, pair(use)[:, 0:4], bias, ALU.add))
                    if e == 0:
                        for use in m.comb:
                            wait_emptied(ve, use)
                    if e >= 2:
                        ve.wait_ge(chunk_done, chunks + (m.down[e - 2] + 1))
                    row = comb[:, e, :] if t is None else comb[:, bass.ds(t * step + e, 1), :].rearrange(
                        "p a t -> p (a t)")
                    V.tensor_tensor(gated[:, at], prod, spread(row, 1, 4), ALU.mult).then_inc(gated_ready, 1)

                for e in range(peeled):
                    one(e)
                chunks = m.gate[peeled + step].chunk - m.gate[peeled].chunk
                uses = m.gate[peeled + step].u - m.gate[peeled].u
                with ve.Fori(0, (EXPERTS - peeled) // step) as t:
                    for i in range(step):
                        one(peeled + i, t, t * chunks, t * (uses // 2))
                update(m.update, m.down[-1], 1)

            def mlp(m, layer):
                norm(m.norm, cols[:, N2_G + layer * KD:N2_G + (layer + 1) * KD])

                def one(j, chunks=0, uses=0):
                    wait_emptied(ve, m.up[j], uses)
                    at = (m.first + j) % 2
                    if j >= 2:
                        ve.wait_ge(chunk_done, chunks + (m.down[j - 2] + 1))
                    V.tensor_tensor(gated[:, at], act[:, at], act[:, at], ALU.mult).then_inc(gated_ready, 1)
                one(0)
                one(1)
                with ve.Fori(0, (FF_PARTS - 2) // 2) as t:
                    for i in range(2):
                        one(2 + i, t * 4, t)
                update(m.update, m.down[-1])

            def rotate(dst, use, c):
                wait_full(ve, use)
                ps = pair(use)[:, :].rearrange("p (h i t) -> p h i t", h=2, i=2)
                cos, sin = spread(rotary[:, 0, :], 1, 2), spread(rotary[:, 1, :], 1, 2)
                d = dst[:, 4 * c:4 * c + 4, :].rearrange("p (h i) t -> p h i t", i=2)
                V.tensor_tensor(r_tmp[:, 0], cos, ps[:, :, 0, :], ALU.mult)
                link(V.tensor_tensor(r_tmp[:, 1], sin, ps[:, :, 1, :], ALU.mult))
                link(V.tensor_tensor(d[:, :, 0, :], r_tmp[:, 0], r_tmp[:, 1], ALU.subtract))
                V.tensor_tensor(r_tmp[:, 0], sin, ps[:, :, 0, :], ALU.mult)
                link(V.tensor_tensor(r_tmp[:, 1], cos, ps[:, :, 1, :], ALU.mult))
                empties(use, V.tensor_tensor(d[:, :, 1, :], r_tmp[:, 0], r_tmp[:, 1], ALU.add))
                wait_emptied(ve, use)

            def retention(r, layer):
                norm(r.norm, cols[:, N1_G + layer * KD:N1_G + (layer + 1) * KD])
                for c in range(4):
                    rotate((r_qT, r_kT)[c // 2], r.proj[c], c % 2)

                def start(h):
                    use = r.scores[h]
                    wait_full(ve, use)
                    sT = r_s[:, h % 2]
                    V.tensor_tensor(sT[:, 0:S], decay[:, h, :], pair(use)[:, 0:S], ALU.mult)
                    empties(use, V.tensor_tensor(sT[:, S:S + P], decay[:, h, 0:P], pair(use)[:, 512:512 + P], ALU.mult))

                def finish(h):
                    ve.wait_ge(rs_ready, r.stat[h] + 1)
                    if h == 0:
                        wait_emptied(ve, r.proj[11])
                    o = tokpair(Y[:, (h % 2) * 1024:(h % 2 + 1) * 1024])
                    vs = slice(h * RDV, (h + 1) * RDV)
                    for b in range(TB):
                        last = V.scalar_tensor_tensor(r_o[:, b, vs], o[:, b, :], rs[:, r.stat[h] % 2, b:b + 1],
                                                      r_g[:, b, vs], ALU.mult, ALU.mult)
                    last.then_inc(r_taken, 1)

                start(0)
                for h in range(RH):
                    if h + 1 < RH:
                        start(h + 1)
                    finish(h)
                for j in (0, 2):
                    use = r.oT[j]
                    wait_full(ve, use)
                    empties(use, V.tensor_copy(r_oT[:, 4 * j:4 * j + 4, :], quads(pair(use)[:, :])))
                update(r.update, r.wo[3])

            ve.wait_ge(const_loaded, 16 * N_CONST)
            wait_full(ve, plan.columns)
            empties(plan.columns, V.tensor_copy(cols[:], pair(plan.columns)[:, 0:2 * P]))
            V.memset(rel_rows[:, S:384], NEG)
            wait_full(ve, plan.rel)
            empties(plan.rel, V.tensor_copy(rel_rows[:, 0:S], pair(plan.rel)[0:16, 0:S]))
            l4 = lam_in.rearrange("p (i j d) -> p i j d", i=2, j=2)
            link(V.tensor_tensor(lam_prod.rearrange("p (i d) -> p i d", i=2), l4[:, :, 0, :], l4[:, :, 1, :], ALU.mult))
            V.tensor_reduce(lam[:, 0:2], lam_prod.rearrange("p (i d) -> p i d", i=2), X, ALU.add).then_inc(lam_ready, 1)
            ve.wait_ge(lam_ready, 2)
            link(V.tensor_tensor(lam[:, 4:5], lam[:, 3:4], lam[:, 2:3], ALU.subtract))
            link(V.tensor_scalar(lam[:, 5:6], lam[:, 4:5], LAMBDA_INIT, None, ALU.subtract))
            link(V.tensor_copy(pos_f[:], pos_i[:]))
            for b in range(TB):
                link(V.tensor_scalar(ropew[:, 0, b, :], inv_rope, pos_f[:, b:b + 1], None, ALU.mult))
            link(V.tensor_copy(ropew[:, 1], ropew[:, 0]))
            TURN = 2.0 * np.pi
            ROUND = 1.5 * 2.0 ** 23
            link(V.tensor_scalar(rope[:, 0], ropew[:, 0], 1.0 / TURN, None, ALU.mult))
            link(V.tensor_scalar(rope[:, 1], ropew[:, 0], 1.0 / TURN, 0.25, ALU.mult, ALU.add))
            link(V.tensor_scalar(rope[:], rope[:], ROUND, None, ALU.add))
            link(V.tensor_scalar(rope[:], rope[:], ROUND, None, ALU.subtract))
            C1 = 6.28125
            C2 = float(np.float32(np.round((TURN - C1) * 2 ** 22) / 2 ** 22))
            C3 = float(np.float32(TURN - C1 - C2))
            for part in (C1, C2, C3):
                link(V.scalar_tensor_tensor(ropew[:], rope[:], -part, ropew[:], ALU.mult, ALU.add))
            link(V.tensor_scalar(ropew[:, 1], ropew[:, 1], float(np.pi / 2), None, ALU.add))
            V.tensor_scalar(ropew[:], ropew[:], 3.1415925, -3.1415925, ALU.min, ALU.max).then_inc(turns_ready, 1)
            for j, use in enumerate(plan.mod_a):
                modulation(use, 4 * j)
                wait_emptied(ve, use)
            gain_of(A_G, SC1)
            norm(plan.a_norm, gain, SH1)
            wait_full(ve, plan.f_logit)
            empties(plan.f_logit, V.tensor_tensor(
                cumq[:], spread(b_f[:, :], 1, TB),
                pair(plan.f_logit)[:, 0:TB * HEADS].rearrange("p (b h) -> p b h", b=TB), ALU.add))
            c = 4
            for j in range(6):
                if j == 0:
                    ve.wait_ge(softplus_ready, 1)
                    V.scalar_tensor_tensor(logf[:], cumq[:], 0.0, logw[:], ALU.min, ALU.subtract).then_inc(logf_ready, 1)
                for use in plan.a_mods[j]:
                    modulation(use, 4 * c)
                    c += 1
                if j == 0:
                    use = plan.cum_q
                    wait_full(ve, use)
                    empties(use, V.tensor_copy(cumq[:], pair(use)[:, 0:TB * HEADS].rearrange("p (b h) -> p b h", b=TB)))
                    wait_emptied(ve, use)
                    for g, use in enumerate(plan.cum_k):
                        wait_full(ve, use)
                        ps = quads(pair(use)[:, :])
                        for i in range(4):
                            h = 4 * g + i
                            V.scalar_tensor_tensor(bias0[:, h, :], causal[:, P:S], cumq[:, 0, h:h + 1],
                                                   ps[:, i, 0:P], ALU.add, ALU.subtract)
                            last = V.scalar_tensor_tensor(bias1[:, h, :], causal, cumq[:, 1, h:h + 1],
                                                          ps[:, i, :], ALU.add, ALU.subtract)
                        empties(use, last)
                        wait_emptied(ve, use)

            attention(plan.att_a, HD, HD ** -0.5,
                      lambda g, qb: (bias0, bias1)[qb][:, 4 * g:4 * g + 4, :])
            update(plan.att_a.update, plan.att_a.wo[1], 0)
            experts(plan.moe0, 1, 0, 4, 2)
            wait_emptied(ve, plan.moe0.mod[-1])
            gain_of(KV_G, MOD["kv"] + KD)
            norm(plan.kv_norm, gain, MOD["kv"])
            ve.wait_ge(rs_ready, plan.kv_stat + 1)
            ve.wait_ge(rope_ready, 1)
            for b in range(TB):
                last = V.tensor_scalar(ckv[:, b, 0:KV_RANK], ckv[:, b, 0:KV_RANK],
                                       rs[:, plan.kv_stat % 2, b:b + 1], None, ALU.mult)
            last.then_inc(latent_ready, 1)
            use = plan.ckvT
            wait_full(ve, use)
            for k in range(2):
                last = V.tensor_scalar(ckvT[:, k, :], quads(pair(use)[:, :])[:, k, :], cols[:, LAT_G + k:LAT_G + k + 1],
                                       None, ALU.mult)
            empties(use, last)

            def rope_of(x1, x2, y1, y2, n):
                sin = spread(rope[:, 0], 2, n)
                cos = spread(rope[:, 1], 2, n)
                r4 = [rot[:, i, 0:TB * n * 16].rearrange("p (b h d) -> p b h d", b=TB, h=n) for i in range(4)]
                link(V.tensor_tensor(r4[0], x1, cos, ALU.mult))
                link(V.tensor_tensor(r4[1], x2, sin, ALU.mult))
                link(V.tensor_tensor(r4[2], x2, cos, ALU.mult))
                link(V.tensor_tensor(r4[3], x1, sin, ALU.mult))
                link(V.tensor_tensor(y1, r4[0], r4[1], ALU.subtract))
                return V.tensor_tensor(y2, r4[2], r4[3], ALU.add)

            kr = ckv[:, :, KV_RANK:KV_RANK + ROPE].unsqueeze(2)
            link(rope_of(kr[:, :, :, 0:16], kr[:, :, :, 16:32], kr[:, :, :, 0:16], kr[:, :, :, 16:32], 1))
            k4 = tokpair(k_area).rearrange("p b (h n) -> p b h n", h=HEADS)
            for b in range(TB):
                link(V.tensor_copy(k4[:, b, :, NOPE:QK_B], spread(ckv[:, b, KV_RANK:KV_RANK + ROPE], 1, HEADS)))
            gain_of(B_G, MOD[1] + SC1)
            norm(plan.b_norm, gain, MOD[1] + SH1)
            ve.wait_ge(rs_ready, plan.cq_stat + 1)
            for b in range(TB):
                last = V.tensor_scalar(cq[:, b, :], cq[:, b, :], rs[:, plan.cq_stat % 2, b:b + 1], None, ALU.mult)
            last.then_inc(latent_ready, 1)
            for j, use in enumerate(plan.cqT):
                wait_full(ve, use)
                n = 4 if j == 0 else 2
                for k in range(n):
                    last = V.tensor_scalar(cqT[:, 4 * j + k, :], quads(pair(use)[:, :])[:, k, :],
                                           cols[:, BQ_G + 4 * j + k:BQ_G + 4 * j + k + 1], None, ALU.mult)
                empties(use, last)
            for use in plan.uq:
                wait_emptied(ve, use)
            q4 = tokpair(q_area).rearrange("p b (h n) -> p b h n", h=HEADS)
            q1, q2 = q4[:, :, :, NOPE:NOPE + 16], q4[:, :, :, NOPE + 16:QK_B]
            rope_of(q1, q2, q1, q2, HEADS).then_inc(qk_ready, 1)
            attention(plan.att_b, QK_B, QK_B ** -0.5,
                      lambda g, qb: spread(chunked[:, P:S] if qb == 0 else chunked, 1, 4))
            update(plan.att_b.update, plan.att_b.wo[1], 0)
            experts(plan.moe1, 2, 1, 4, 4)
            ve.wait_ge(rs_ready, plan.final_stat + 1)
            ve.wait_ge(gain_loaded, 16)
            for b in range(TB):
                V.scalar_tensor_tensor(x[:, b, :], x[:, b, :], rs[:, plan.final_stat % 2, b:b + 1], gates[:, 0, :],
                                       ALU.mult, ALU.mult).then_inc(updated, 1)
            retention(plan.ret0, 0)
            mlp(plan.mlp0, 0)

            def softmax_layer(a, nth, layer):
                norm(a.norm, cols[:, N1_G + layer * KD:N1_G + (layer + 1) * KD])
                sq = o_flat
                for i, area in enumerate((q_area[:, 0:2048], k_area[:, 0:2048])):
                    for use in a.proj[2 * i:2 * i + 2]:
                        wait_emptied(ve, use)
                    link(V.tensor_tensor(sq, area, area, ALU.mult))
                    V.tensor_reduce(ss[:, a.qk_stat[i] % 2, 0:32], sq.rearrange("p (h d) -> p h d", d=HD), X,
                                    ALU.add).then_inc(squared, 1)
                    ve.wait_ge(rs_ready, a.qk_stat[i] + 1)
                    heads = area.rearrange("p (h d) -> p h d", d=HD)
                    last = V.tensor_tensor(heads, heads, spread(rs[:, a.qk_stat[i] % 2, 0:32], 2, HD), ALU.mult)
                last.then_inc(qk_ready, 1)
                if nth == 0:
                    ve.wait_ge(rel_loaded, 16)
                attention(a.att, HD, HD ** -0.5,
                          lambda g, qb: relbias[:, 4 * g:4 * g + 4, P:S] if qb == 0 else relbias[:, 4 * g:4 * g + 4, :],
                          k_scale=head_gain[0:HD, 2 * nth + 1:2 * nth + 2], diff=a.diff,
                          subln_stat=a.o_stat if a.diff else None)
                update(a.att.update, a.att.wo[1])

            softmax_layer(plan.moba, 0, 1)
            mlp(plan.mlp1, 1)
            softmax_layer(plan.diff, 1, 2)
            mlp(plan.mlp2, 2)
            retention(plan.ret1, 3)
            mlp(plan.mlp3, 3)


_INS = ["x", "c", "positions", "a_norm_g", "a_w_in", "a_b_f", "a_w_o", "kv_norm_g", "kv_w_mod", "kv_b_mod",
        "kv_w_down", "kv_latent_g", "kv_w_up", "b_norm_g", "b_w_dq", "b_q_norm_g", "b_w_uq", "b_w_o", "w_mod",
        "b_mod", "ffn_norm_g", "router_w", "router_bias", "exp_w_gate", "exp_w_up", "exp_w_down", "final_norm_g",
        "rel_bias_2", "norm1_2", "norm2_2", "w_up_2", "w_down_2", "ret_w_in_2", "ret_w_out_2", "moba_w_in_2",
        "moba_q_norm_2", "moba_k_norm_2", "moba_w_out_2", "diff_w_in_2", "diff_q_norm_2", "diff_k_norm_2",
        "diff_lambda_2", "diff_subln_2", "diff_w_out_2"]


def kernel(**inputs):
    import concourse.bacc as bacc
    from concourse.bass_utils import run_bass_kernel_spmd

    nc = bacc.Bacc("TRN2", target_bir_lowering=False, num_devices=1)
    arrays = {}

    def dram(name, a):
        arrays[name] = a
        return nc.dram_tensor(name, a.shape, mybir.dt.from_np(a.dtype), kind="ExternalInput").ap()

    w = {name: dram(f"in_{name}", np.ascontiguousarray(inputs[name])) for name in _INS}
    table = {name: dram(f"table_{name}", a) for name, a in shape_constants().items()}
    out = nc.dram_tensor("out", (1, S, D), F32, kind="ExternalOutput").ap()
    rel_scratch = nc.dram_tensor("rel_scratch", (HEADS, P, 384), F32, kind="Internal").ap()
    build(nc, w, table, out, rel_scratch)
    return run_bass_kernel_spmd(nc, [arrays], core_ids=[0]).results[0]["out"]
```

```python
from contextlib import ExitStack

import numpy as np

import concourse.bass as bass
from concourse import mybir

F32 = mybir.dt.float32
F32R = mybir.dt.float32r
I32 = mybir.dt.int32
ALU = mybir.AluOpType
ACT = mybir.ActivationFunctionType
X = mybir.AxisListType.X

P = 128
S = 256
TB = S // P
D = 1024
KD = D // P
HEADS = 16
HD = D // HEADS
NOPE, ROPE = 64, 32
QK_B = NOPE + ROPE
Q_RANK, KV_RANK = 768, 256
CHUNK_B = 64
EXPERTS, GROUPS = 16, 4
PER_GROUP = EXPERTS // GROUPS
DE = 512
D_FF = 4 * D
FF_PARTS = D_FF // DE
RH, RDK, RDV = 4, 256, 512
RET_IN = 2 * RH * RDK + 2 * RH * RDV
EPS = 1e-6
NEG = -1e30
RING = 3
PIECE = 2048

FIRST_MODS = 4
LAYER_MODS = 12

LAMBDA_INIT = 0.8 - 0.6 * float(np.exp(-0.3 * 2))


def shape_constants():
    f = np.float32
    q = np.arange(P)[:, None]
    c = np.arange(S)[None, :]
    dist = q + P - c
    causal = np.where(dist >= 0, f(0), f(NEG)).astype(f)
    chunked = np.where((q + P) // CHUNK_B >= c // CHUNK_B, f(0), f(NEG)).astype(f)
    ident = np.eye(P, dtype=f)
    upto = (np.arange(P)[:, None] <= np.arange(P)[None, :]).astype(f)
    lg = np.log(f(1.0) - f(2.0) ** (f(-5.0) - np.arange(RH, dtype=f))).astype(f)
    rel = np.arange(S)[None, :] - np.arange(P)[:, None]
    decay = np.where(rel[:, None, :] >= 0,
                     np.exp(np.maximum(rel, 0).astype(f)[:, None, :] * lg[None, :, None]), f(0)).astype(f)
    decay = decay * f(RDK ** -0.5)
    inv = (f(10000.0) ** (-np.arange(0, RDK, 2, dtype=f) / f(RDK))).astype(f)
    ang = (inv[:, None] * np.arange(S, dtype=f)[None, :]).astype(f)
    half = ROPE // 2
    inv_rope = (f(10000.0) ** (-np.arange(half, dtype=f) / f(half))).astype(f)
    n = (S - 1 - np.arange(S))
    large = 16 + (np.log(np.maximum(n, 1).astype(f) / f(16)) / f(np.log(64.0)) * f(16)).astype(np.int32)
    bucket = np.where(n < 16, n, np.minimum(large, 31))
    onehot = (np.arange(32)[:, None] == bucket[None, :]).astype(f)
    return {
        "squares": np.concatenate([ident, upto], 1),
        "masks": np.concatenate([causal, chunked], 1),
        "decay": np.ascontiguousarray(decay.reshape(P, RH * S)),
        "rotary": np.concatenate([np.cos(ang), np.sin(ang)], 1).astype(f),
        "small": np.tile(np.concatenate([inv_rope, np.array([4, 3, 2, 1], f)])[None, :], (P, 1)),
        "onehot": onehot,
    }


def head_at(i):
    return (0, 2, 1, 3)[i]


class Use:

    def __init__(self, u, chunk=None, fill=None):
        self.u, self.chunk, self.fill = u, chunk, fill


class Plan:

    def __init__(self):
        self.n = {}
        self.stats = []
        self.streamed = []
        self.sizes = []

    def take(self, what, k=1):
        at = self.n.get(what, 0)
        self.n[what] = at + k
        return at

    def fills(self, k):
        return [Use(self.take("use"), fill=self.take("fill")) for _ in range(k)]

    def chunk(self, *what, size=PIECE):
        self.streamed.append(what)
        self.sizes += [size, size]
        return self.take("chunk")

    def proj(self, *what, size=PIECE):
        return Use(self.take("use"), chunk=self.chunk(*what, size=size))

    def mods(self, k):
        return [(self.take("mod"), use) for use in self.fills(k)]

    def stat(self, cols, length):
        self.stats.append((cols, 1.0 / length))
        return self.take("stat")


class Phase:
    pass


def norm_plan(p, after, late=False, again=False):
    n = Phase()
    n.after, n.late, n.again = after, late, again
    if not again:
        n.stat = p.stat(TB, D)
    if again:
        n.scaled = p.n["scaled"] - 1
    elif late:
        n.kept = p.take("kept")
    else:
        n.scaled = p.take("scaled")
    n.uses = p.fills(2)
    n.high = p.take("high", 2)
    n.feed = 2 * p.n.get("chunk", 0) + RING
    return n


def attention_plan(p, wo, packed=True):
    a = Phase()
    a.packed = packed
    a.kq = p.fills(4 if packed else 2 * HEADS // 4)
    a.unit = p.take("unit", 2 * HEADS // 4)
    a.scores = p.fills(2 * HEADS // 4)
    a.oT = p.fills(2)
    a.high = p.take("high", 2)
    a.wo = [p.chunk("rows", wo, j) for j in range(2)]
    a.update = p.take("update")
    return a


def experts_plan(p, layer, mods):
    m = Phase()
    m.norm = norm_plan(p, p.n["update"])
    m.router = p.fills(1)[0]
    m.first = p.take("gated", EXPERTS)
    m.gate, m.up, m.down, m.mod = [], [], [], []
    for e in range(EXPERTS):
        m.gate.append(p.proj("cols", "exp_w_gate", (layer, e), 0))
        m.up.append(p.proj("cols", "exp_w_up", (layer, e), 0))
        if e:
            m.down.append(p.chunk("rows_e", "exp_w_down", (layer, e - 1)))
        if mods:
            m.mod += p.mods(1)
        if e == 0:
            m.comb = p.fills(EXPERTS // 4)
    m.down.append(p.chunk("rows_e", "exp_w_down", (layer, EXPERTS - 1)))
    m.update = p.take("update")
    return m


def mlp_plan(p, layer):
    m = Phase()
    m.norm = norm_plan(p, p.n["update"], late=True)
    m.first = p.take("gated", FF_PARTS)
    m.up, m.down = [], []
    for j in range(FF_PARTS):
        m.up.append(p.proj("cols", "w_up_2", layer, j))
        if j:
            m.down.append(p.chunk("rows", ("w_down_2", layer), j - 1))
    m.down.append(p.chunk("rows", ("w_down_2", layer), FF_PARTS - 1))
    m.update = p.take("update")
    return m


def retention_plan(p, j):
    r = Phase()
    r.norm = norm_plan(p, p.n["update"])
    r.proj = [p.proj("cols" if c < 4 else "tok", "ret_w_in_2", j, c) for c in range(RET_IN // 512)]
    r.scores = p.fills(RH)
    r.head = p.take("head", RH)
    r.stat = [p.stat(TB, RDV) for _ in range(RH)]
    r.oT = p.fills(4)
    r.high = p.take("high", 4)
    r.wo = [p.chunk("rows", ("ret_w_out_2", j), c) for c in range(RH * RDV // 512)]
    r.update = p.take("update")
    return r


def softmax_layer_plan(p, name, diff):
    a = Phase()
    a.norm = norm_plan(p, p.n["update"], late=True)
    a.proj = [p.proj("tok", name + "_w_in_2", 0, c) for c in range(6)]
    a.qk_stat = [p.stat(TB * HEADS, HD) for _ in range(2)]
    a.qk_normed = p.take("qk_normed", 2)
    a.diff = diff
    att = attention_plan(p, (name + "_w_out_2", 0))
    if diff:
        a.o_stat = p.stat(TB * HEADS // 2, 2 * HD)
    a.att = att
    return a


def make_plan():
    p = Plan()
    p.n["update"] = 0
    p.columns, p.rel = p.fills(2)
    p.mod_a = p.mods(4)
    p.a_norm = norm_plan(p, 0)
    p.f_logit = p.fills(1)[0]
    p.a_proj, p.a_mods, p.cum = [], [], []
    for j in range(6):
        p.a_proj.append(p.proj("tok", "a_w_in", 0, j))
        p.cum.append(p.fills(1)[0] if j < 5 else None)
        p.a_mods.append(p.mods((0, 1, 1, 1, 1, 4)[j]))
    p.gates_a = p.fills(2)
    p.att_a = attention_plan(p, ("a_w_o", 0))
    p.moe0 = experts_plan(p, 0, True)
    p.kv_norm = norm_plan(p, p.n["update"])
    p.kv_down = p.proj("kv_down", size=4 * (KV_RANK + ROPE))
    p.kv_stat = p.stat(TB, KV_RANK)
    p.ckvT = p.fills(1)[0]
    p.ckv_high = p.take("high")
    p.kv_up = [p.proj("kv_up", j, size=512) for j in range(4)]
    p.b_norm = norm_plan(p, p.n["update"], again=True)
    p.dq = [p.proj("tok", "b_w_dq", 0, 0), p.proj("dq_tail", size=1024)]
    p.cq_stat = p.stat(TB, Q_RANK)
    p.cqT = p.fills(2)
    p.cq_high = p.take("high", 2)
    p.uq = [p.proj("uq", j, size=3 * 512) for j in range(3)]
    p.gates_b = p.fills(2)
    p.att_b = attention_plan(p, ("b_w_o", 0), packed=False)
    p.moe1 = experts_plan(p, 1, False)
    p.final_stat = p.stat(TB, D)
    p.final_update = p.take("update")
    p.ret0 = retention_plan(p, 0)
    p.mlp0 = mlp_plan(p, 0)
    p.moba = softmax_layer_plan(p, "moba", False)
    p.mlp1 = mlp_plan(p, 1)
    p.diff = softmax_layer_plan(p, "diff", True)
    p.mlp2 = mlp_plan(p, 2)
    p.ret1 = retention_plan(p, 1)
    p.mlp3 = mlp_plan(p, 3)
    return p


def spread(ap, axis, n):
    shape = list(ap.shape)
    return ap.unsqueeze(axis).to_broadcast(shape[:axis] + [n] + shape[axis:])




def build(nc, w, table, out, rel_scratch):
    plan = make_plan()
    ctx = ExitStack()
    with ctx:
        def sb(name, shape, dt=F32):
            return ctx.enter_context(nc.sbuf_tensor(name, shape, dt))

        def sem(name):
            return ctx.enter_context(nc.semaphore(name))

        raw = sb("raw", [P, RING, PIECE])
        w_high = sb("w_high", [P, RING, PIECE], F32R)
        w_low = sb("w_low", [P, RING, PIECE], F32R)
        x = sb("x", [P, TB, D])
        hT_high = sb("hT_high", [P, KD, S], F32R)
        hT_low = sb("hT_low", [P, KD, S], F32R)
        gated_high = sb("gated_high", [P, 2, 4, S], F32R)
        gated_low = sb("gated_low", [P, 2, 4, S], F32R)
        thin_high = sb("thin_high", [P, 2, KD, 16], F32R)
        thin_low = sb("thin_low", [P, 2, KD, 16], F32R)
        gates = sb("gates", [P, 2, D])
        squares = sb("squares", [P, 2 * P])
        masks = sb("masks", [P, 2 * S])
        rotary = sb("rotary", [P, 2, S])
        small = sb("small", [P, ROPE // 2 + PER_GROUP])
        cols = sb("cols", [P, 2 * P])
        mod = sb("mod", [P, 112])
        head_gain = sb("head_gain", [P, 4])
        subln = sb("subln", [P, 1])
        b_f = sb("b_f", [P, HEADS])
        r_bias = sb("r_bias", [P, EXPERTS])
        c_act = sb("c_act", [P, KD])
        gain = sb("gain", [P, KD])
        gain_b = sb("gain_b", [P, KD])
        ss = sb("ss", [P, 2, 32])
        rs = sb("rs", [P, 2, 32])
        rs_kept = sb("rs_kept", [P, TB])
        minus_half = sb("minus_half", [P, 32])
        negmax = sb("negmax", [P, 3, 4])
        expsum = sb("expsum", [P, 3, 4])
        recip = sb("recip", [P, 2, 4])
        lam = sb("lam", [P, 8])
        pos_i = sb("pos_i", [P, TB], I32)
        pos_f = sb("pos_f", [P, TB])
        rope = sb("rope", [P, 2, TB, ROPE // 2])
        ropew = sb("ropew", [P, 2, TB, ROPE // 2])
        logf = sb("logf", [P, TB, HEADS])
        logw = sb("logw", [P, TB, HEADS])
        cumq = sb("cumq", [P, TB, HEADS])
        route = sb("route", [P, 10, TB * EXPERTS])
        work = sb("work", [P, 19 * 1024])

        ident, upto_m = squares[:, 0:P], squares[:, P:2 * P]
        ones_col = squares[:, 2 * P - 1:2 * P]
        causal, chunked = masks[:, 0:S], masks[:, S:2 * S]
        inv_rope, descending = small[:, 0:ROPE // 2], small[:, ROPE // 2:]

        xn = work[:, 0:2048].rearrange("p (b n) -> p b n", b=TB)
        xn_tmp = work[:, 2048:4096]

        q_area, k_area = work[:, 0:2048], work[:, 2048:4096]
        v_area = work[:, 5120:7168]
        qT_area, kT_area = work[:, 7168:9216], work[:, 9216:11264]
        o_area = work[:, 11264:13312]
        bias0 = work[:, 13312:15360].rearrange("p (h t) -> p h t", h=HEADS)
        bias1 = work[:, 15360:19456].rearrange("p (h t) -> p h t", h=HEADS)
        relbias = bias1
        probs = work[:, 0:3072].rearrange("p (s h t) -> p s h t", s=3, h=4)
        pT = work[:, 3072:5120].rearrange("p (s h t) -> p s h t", s=2, h=4)
        diff_tmp = work[:, 13312:13824].rearrange("p (j i d) -> p j i d", j=2, i=2)
        b_q, b_k = work[:, 0:3072], work[:, 3072:6144]
        b_v = work[:, 6144:8192]
        b_qT, b_kT = work[:, 8192:12288], work[:, 12288:16384]
        b_o = work[:, 16384:18432]
        ckv = work[:, 8192:8192 + 576].rearrange("p (b n) -> p b n", b=TB)
        cq = work[:, 0:1536].rearrange("p (b n) -> p b n", b=TB)
        rot = work[:, 12288:14336].rearrange("p (i n) -> p i n", i=4)
        b_tmp = work[:, 14336:16384]
        mod_raw = work[:, 7168:11264].rearrange("p (s k n) -> p s k n", s=2, k=4)
        mod_sum = work[:, 11264:13312].rearrange("p (s n) -> p s n", n=512)
        first_raw = work[:, 3072:19456].rearrange("p (s k n) -> p s k n", s=2 * FIRST_MODS, k=4)
        first_sum = gates[:].rearrange("p i (s n) -> p (i s) n", n=512)
        act = work[:, 0:2048].rearrange("p (s f t) -> p s f t", s=2, f=4)
        prod = work[:, 2048:3072].rearrange("p (f t) -> p f t", f=4)
        comb = work[:, 3072:7168].rearrange("p (e t) -> p e t", e=EXPERTS)
        final_gain = work[:, 8192:9216]
        r_qT = work[:, 0:2048].rearrange("p (k t) -> p k t", k=8)
        r_kT = work[:, 2048:4096].rearrange("p (k t) -> p k t", k=8)
        r_v = work[:, 4096:8192].rearrange("p (b n) -> p b n", b=TB)
        r_g = work[:, 8192:12288].rearrange("p (b n) -> p b n", b=TB)
        r_o = work[:, 12288:16384].rearrange("p (b n) -> p b n", b=TB)
        r_tmp = work[:, 16384:17408].rearrange("p (i h t) -> p i h t", i=2, h=2)
        r_s = work[:, 17408:17408 + 768].rearrange("p (s t) -> p s t", s=2)
        decay = work[:, 18432:19456].rearrange("p (h t) -> p h t", h=RH)
        rows = work[:, 0:256]
        rel_in = work[0:32, 256:256 + 16]
        onehot = work[0:32, 512:512 + 256]
        rel_rows = work[0:16, 2304:2304 + 384]
        thin = work[:, 1536:1536 + 256].rearrange("p (i k n) -> p i k n", i=2, k=KD)
        lam_in = work[:, 2048:2048 + 256]
        lam_prod = work[:, 2688:2688 + 128]

        A_G, KV_G, B_G, FFN_G, N1_G, N2_G, C_IN, BQ_G, LAT_G = 0, 8, 16, 24, 40, 72, 104, 112, 118
        MOD_B = P
        MOD = {0: 0, "kv": 48, 1: 64}
        SH1, SC1, G1, SH2, SC2, G2 = (k * KD for k in range(6))

        pairs = [ctx.enter_context(nc.psum_tensor(f"pair{i}", [P, 1024], F32)) for i in range(2)]
        Y = ctx.enter_context(nc.psum_tensor("Y", [P, 2048], F32))
        y_sum = Y[:, :].rearrange("p (b n) -> p b n", b=TB)
        pT_ps = Y[:, 0:1024].rearrange("p (h t) -> p h t", h=4)
        o_ps = [Y[:, 1024:1536], Y[:, 1536:2048]]

        rows_loaded = sem("rows_loaded")
        const_loaded = sem("const_loaded")
        x_loaded = sem("x_loaded")
        raw_loaded = [sem(f"raw_loaded{i}") for i in range(RING)]
        high_ready = sem("high_ready")
        low_ready = sem("low_ready")
        piece_done = sem("piece_done")
        fill_done = sem("fill_done")
        first_block_done = sem("first_block_done")
        hT_high_made = sem("hT_high_made")
        product_ready = sem("product_ready")
        gated_high_made = sem("gated_high_made")
        mod_loaded = [sem(f"mod_loaded{i}") for i in range(2)]
        first_loaded = [sem(f"first_loaded{i}") for i in range(2 * FIRST_MODS)]
        mod_step = sem("mod_step")
        thin_high_made = sem("thin_high_made")
        thin_ready = sem("thin_ready")
        emptied = [sem(f"emptied{i}") for i in range(2)]
        lam_ready = sem("lam_ready")
        half_ready = sem("half_ready")
        c_ready = sem("c_ready")
        updated = sem("updated")
        squared = sem("squared")
        mean_ready = sem("mean_ready")
        rs_ready = sem("rs_ready")
        scaled = sem("scaled")
        kept_ready = sem("kept_ready")
        logf_ready = sem("logf_ready")
        masked = sem("masked")
        turns_ready = sem("turns_ready")
        rope_ready = sem("rope_ready")
        softplus_ready = sem("softplus_ready")
        combined = sem("combined")
        gated_ready = sem("gated_ready")
        qk_ready = sem("qk_ready")
        max_ready = sem("max_ready")
        probs_ready = sem("probs_ready")
        pT_done = sem("pT_done")
        pT_ready = sem("pT_ready")
        pv_done = sem("pv_done")
        o_taken = sem("o_taken")
        o_ready = sem("o_ready")
        latent_ready = sem("latent_ready")
        r_pv_done = sem("r_pv_done")
        r_taken = sem("r_taken")
        rel_stored = sem("rel_stored")
        rel_loaded = sem("rel_loaded")
        gain_loaded = sem("gain_loaded")
        decay_loaded = sem("decay_loaded")
        vchain = sem("vchain")
        achain = sem("achain")
        stored = sem("stored")

        def pair(use):
            return pairs[use.u % 2]

        def wait_raw(eng, s, turns=0):
            eng.wait_ge(raw_loaded[s % RING], turns * (16 * TURN_PIECES // RING) + 16 * (s // RING + 1))

        def wait_piece(eng, s, turns=0):
            eng.wait_ge(piece_done, turns * TURN_PIECES + (s + 1))

        def wait_full(eng, use, turns=0):
            if use.chunk is not None:
                wait_piece(eng, 2 * use.chunk + 1, turns)
            else:
                eng.wait_ge(fill_done, turns * 2 + (use.fill + 1))

        def wait_emptied(eng, use, more_uses=0):
            eng.wait_ge(emptied[use.u % 2], more_uses + (use.u // 2 + 1))

        def wait_free(eng, use, more_uses=0):
            if use.u >= 2:
                eng.wait_ge(emptied[use.u % 2], more_uses + use.u // 2)

        def heads_of(area, dh=HD):
            return area.rearrange("p (b h n) -> p b h n", b=TB, n=dh)

        def r_blocks(j):
            if j < 2:
                return hT_high[:, 4 * j:4 * j + 4, :], hT_low[:, 4 * j:4 * j + 4, :]
            return gated_high[:, j - 2], gated_low[:, j - 2]

        def mod_total(m):
            if m < FIRST_MODS:
                return first_sum[:, m]
            return mod_sum[:, m % (4 if m < LAYER_MODS else 2)]

        def wait_mod(eng, m, steps, turns=0):
            eng.wait_ge(mod_step, turns * 16 + (8 * m + steps))

        def quads(ap):
            return ap.rearrange("p (f t) -> p f t", f=4)

        def quads_of(area, j):
            return quads(area[:, 1024 * j:1024 * (j + 1)])

        def tokpair(ap):
            return ap.rearrange("p (b n) -> p b n", b=TB)

        def row_blocks(name, r0, c0, at=None):
            v = w[name]
            v = v.rearrange("l (r c) -> (l r) c", c=P) if len(v.shape) == 2 else v.rearrange("(r c) -> r c", c=P)
            return rows[r0:r0 + v.shape[0], c0:c0 + P], v

        small_loads = [
            (squares[:], table["squares"]),
            row_blocks("a_norm_g", A_G, 0), row_blocks("kv_norm_g", KV_G, 0), row_blocks("b_norm_g", B_G, 0),
            row_blocks("ffn_norm_g", FFN_G, 0), row_blocks("norm1_2", N1_G, 0), row_blocks("norm2_2", N2_G, 0),
            row_blocks("c", C_IN, 0), row_blocks("b_q_norm_g", BQ_G, 0), row_blocks("kv_latent_g", LAT_G, 0),
            (rows[120:P, 0:P], table["squares"][0:P - 120, 0:P]),
            (rows[0:48, P:2 * P], w["b_mod"][0].rearrange("(r c) -> r c", c=P)),
            row_blocks("kv_b_mod", 48, P),
            (rows[64:112, P:2 * P], w["b_mod"][1].rearrange("(r c) -> r c", c=P)),
            (rows[112:P, P:2 * P], table["squares"][0:P - 112, 0:P]),
        ]
        early = len(small_loads)
        small_loads += [
            (onehot, table["onehot"]),
            (lam_in, w["diff_lambda_2"].rearrange("l i d -> l (i d)").to_broadcast([P, 256])),
            (pos_i[:], w["positions"].rearrange("o (b p) -> p (o b)", p=P)),
            (small[:], table["small"]), (masks[:], table["masks"]),
            (thin[:, 0], w["a_w_in"][0].rearrange("(k p) n -> p k n", p=P)[:, :, 3 * D:3 * D + HEADS]),
            (b_f[:], w["a_b_f"].to_broadcast([P, HEADS])),
            (thin[:, 1], w["router_w"].rearrange("(k p) n -> p k n", p=P)),
            (r_bias[:], w["router_bias"].unsqueeze(0).to_broadcast([P, EXPERTS])),
            (rotary[:].rearrange("p i t -> p (i t)"), table["rotary"]),
            (subln[:], w["diff_subln_2"].rearrange("l (d o) -> d (l o)", o=1)),
        ] + [
            (rel_in.rearrange("n (g i) -> n g i", i=4)[:, :, i:i + 1],
             w["rel_bias_2"].rearrange("n (g i) -> n g i", i=4)[:, :, head_at(i):head_at(i) + 1]) for i in range(4)
        ] + [(head_gain[half:half + HD, i:i + 1], w[name].rearrange("l (d o) -> d (l o)", o=1))
             for half in (0, HD) for i, name in enumerate(
                 ("moba_q_norm_2", "moba_k_norm_2", "diff_q_norm_2", "diff_k_norm_2"))]
        N_CONST = len(small_loads) - early

        TURNS = (EXPERTS - 2) // 2
        TURN_PIECES = 12
        TURN_USES = {False: 2, True: 3}

        block = ctx.enter_context(nc.Block())

        @block.sync
        def _(sp):
            def source(what):
                kind = what[0]
                if kind in ("cols", "tok"):
                    _, name, at, j = what
                    m = w[name]
                    m = m[at[0], at[1]] if isinstance(at, tuple) else m[at]
                    return m.rearrange("(k p) n -> p k n", p=P)[:, :, j * 512:(j + 1) * 512]
                if kind == "rows":
                    _, (name, at), j = what
                    return w[name][at, j * 512:(j + 1) * 512, :].rearrange("(k p) n -> p k n", p=P)
                if kind == "rows_e":
                    _, name, (layer, e) = what
                    return w[name][layer, e].rearrange("(k p) n -> p k n", p=P)
                if kind == "kv_down":
                    return w["kv_w_down"].rearrange("(k p) n -> p k n", p=P)
                if kind == "kv_up":
                    return w["kv_w_up"].rearrange("(k p) n -> p k n", p=P)[:, :, what[1] * 512:(what[1] + 1) * 512]
                if kind == "dq_tail":
                    return w["b_w_dq"][0].rearrange("(k p) n -> p k n", p=P)[:, :, 512:768]
                if kind == "uq":
                    return w["b_w_uq"][0].rearrange("(k p) n -> p k n", p=P)[:, :, what[1] * 512:(what[1] + 1) * 512]

            def load(c, src, turns=0, by_columns=False):
                k, n = src.shape[1], src.shape[2]
                for h in range(2):
                    s = 2 * c + h
                    part = src[:, :, h * (n // 2):(h + 1) * (n // 2)] if by_columns else src[:, h * (k // 2):(h + 1) * (k // 2)]
                    if s >= RING:
                        sp.wait_ge(low_ready, turns * TURN_PIECES + (s - RING + 1))
                    kk, nn = part.shape[1], part.shape[2]
                    dst = raw[:, s % RING, 0:kk * nn].rearrange("p (k n) -> p k n", k=kk)
                    sp.dma_start(dst, part).then_inc(raw_loaded[s % RING], 16)

            def load_range(a, b):
                for c in range(a, b):
                    load(c, source(plan.streamed[c]), by_columns=plan.streamed[c][0] == "cols")

            def load_experts(m, layer):
                with sp.Fori(0, TURNS) as t:
                    for i in range(2):
                        e = t * 2 + (2 + i)
                        load(m.gate[2 + i].chunk, w["exp_w_gate"][layer, bass.ds(e, 1)]
                             .rearrange("e (k p) n -> p (e k) n", p=P), t, True)
                        load(m.up[2 + i].chunk, w["exp_w_up"][layer, bass.ds(e, 1)]
                             .rearrange("e (k p) n -> p (e k) n", p=P), t, True)
                        load(m.down[1 + i], w["exp_w_down"][layer, bass.ds(t * 2 + (1 + i), 1)]
                             .rearrange("e (k p) n -> p (e k) n", p=P), t)

            sp.wait_ge(rows_loaded, 16 * early)
            for dst, src in small_loads[early:]:
                sp.dma_start(dst, src, allow_slow_non_contiguous=True).then_inc(const_loaded, 16)
            sp.wait_ge(first_loaded[5], 16)
            load_range(0, plan.moe0.gate[2].chunk)
            load_experts(plan.moe0, 0)
            load_range(plan.moe0.down[-1], plan.moe1.gate[2].chunk)
            load_experts(plan.moe1, 1)
            load_range(plan.moe1.down[-1], len(plan.streamed))
            for b in range(TB):
                sp.wait_ge(updated, TB * plan.mlp3.update + b + 1)
                sp.dma_start(out[0, b * P:(b + 1) * P, :], x[:, b, :]).then_inc(stored, 16)
            sp.wait_ge(stored, 16 * TB)

        @block.gpsimd
        def _(pool):
            nc.gpsimd.memset(minus_half[:], -0.5).then_inc(half_ready, 1)

            def load_mod(m, h, src, turns=0):
                before = m - 1 if m > FIRST_MODS else 1
                wait_mod(pool, before, 4 * h + 4, turns)
                pool.dma_start(mod_raw[:, h], src[:, 4 * h:4 * h + 4]).then_inc(mod_loaded[h], 16)

            def columns(name, layer=None):
                m = w[name] if layer is None else w[name][layer]
                return m.rearrange("(k p) n -> p k n", p=P)

            def inverse_rms(r):
                n, inv = plan.stats[r]
                pool.wait_ge(squared, r + 1)
                v = ss[:, r % 2, 0:n]
                nc.gpsimd.tensor_scalar(v, v, inv, EPS, ALU.mult, ALU.add).then_inc(mean_ready, 1)
                pool.wait_ge(mean_ready, r + 1)
                nc.gpsimd.tensor_tensor(rs[:, r % 2, 0:n], v, minus_half[:, 0:n], ALU.pow).then_inc(rs_ready, 1)

            def layer_mod(c):
                return columns("w_mod", 0)[:, :, c * 512:(c + 1) * 512]

            for i in range(2 * FIRST_MODS):
                if i == 3:
                    pool.wait_ge(rows_loaded, 16 * early)
                pool.dma_start(first_raw[:, i], layer_mod(i // 2)[:, 4 * (i % 2):4 * (i % 2) + 4]).then_inc(first_loaded[i], 16)
            for h in range(2):
                load_mod(FIRST_MODS, h, layer_mod(FIRST_MODS))
            pool.wait_ge(half_ready, 1)
            inverse_rms(plan.a_norm.stat)
            for c in range(FIRST_MODS + 1, LAYER_MODS):
                for h in range(2):
                    load_mod(c, h, layer_mod(c))
                if c == LAYER_MODS - 2:
                    wait_emptied(pool, plan.cum[4])
                    for bias, mask in ((bias0, causal[:, P:S]), (bias1, causal)):
                        nc.gpsimd.tensor_tensor(bias, bias, spread(mask, 1, HEADS), ALU.add).then_inc(masked, 1)
            inverse_rms(plan.moe0.norm.stat)
            pool.dma_start(work[:, 18432:19456], table["decay"]).then_inc(decay_loaded, 16)
            for c in range(4):
                for h in range(2):
                    load_mod(LAYER_MODS + c, h, columns("kv_w_mod")[:, :, c * 512:(c + 1) * 512])
            with pool.Fori(0, LAYER_MODS // 2) as t:
                for i in range(2):
                    for h in range(2):
                        load_mod(16 + i, h, columns("w_mod", 1)[:, :, bass.ds(t * 1024 + i * 512, 512)], t)
            for r in range(plan.kv_norm.stat, len(plan.stats)):
                inverse_rms(r)
                if r == plan.mlp2.norm.stat:
                    pool.dma_start(work[:, 18432:19456], table["decay"]).then_inc(decay_loaded, 16)

        @block.tensor
        def _(pe):
            def piece(ring, s, k, n):
                return ring[:, s % RING, 0:k * n].rearrange("p (k n) -> p k n", k=k)

            def wait_high(s, turns=0):
                pe.wait_ge(high_ready, turns * TURN_PIECES + (s + 1))

            def wait_low(s, turns=0):
                pe.wait_ge(low_ready, turns * TURN_PIECES + (s + 1))

            def transposed_product(use, turns=0, more_uses=0):
                ps = quads(pair(use)[:, :])
                wait_free(pe, use, more_uses)
                for j in range(2):
                    s = 2 * use.chunk + j
                    high, low = piece(w_high, s, KD, 256), piece(w_low, s, KD, 256)
                    wait_high(s, turns)
                    for i in range(2):
                        f, cols_ = 2 * j + i, slice(i * P, (i + 1) * P)
                        for k in range(KD):
                            nc.tensor.matmul(ps[:, f, :], high[:, k, cols_], hT_high[:, k, :], start=(k == 0), stop=False)
                            nc.tensor.matmul(ps[:, f, :], high[:, k, cols_], hT_low[:, k, :], start=False, stop=False)
                        if i == 0:
                            wait_low(s, turns)
                        for k in range(KD):
                            last = nc.tensor.matmul(ps[:, f, :], low[:, k, cols_], hT_high[:, k, :],
                                                    start=False, stop=(k == KD - 1))
                    last.then_inc(piece_done, 1)

            def token_product(use, k_blocks=KD, n=512):
                ps = tokpair(pair(use)[:, :])
                wait_free(pe, use)
                half = k_blocks // 2
                for j in range(2):
                    s = 2 * use.chunk + j
                    high, low = piece(w_high, s, half, n), piece(w_low, s, half, n)
                    wait_high(s)
                    for b in range(TB):
                        bs = slice(b * P, (b + 1) * P)
                        for k in range(half):
                            kk = j * half + k
                            nc.tensor.matmul(ps[:, b, 0:n], hT_high[:, kk, bs], high[:, k, :], start=(kk == 0), stop=False)
                            nc.tensor.matmul(ps[:, b, 0:n], hT_low[:, kk, bs], high[:, k, :], start=False, stop=False)
                    wait_low(s)
                    for b in range(TB):
                        for k in range(half):
                            kk = j * half + k
                            last = nc.tensor.matmul(ps[:, b, 0:n], hT_high[:, kk, b * P:(b + 1) * P], low[:, k, :],
                                                    start=False, stop=(kk == k_blocks - 1))
                    last.then_inc(piece_done, 1)

            def thin_product(use, which):
                wait_free(pe, use)
                for b in range(TB):
                    bs = slice(b * P, (b + 1) * P)
                    ps = pair(use)[:, b * 16:(b + 1) * 16]
                    for k in range(KD):
                        nc.tensor.matmul(ps, hT_high[:, k, bs], thin_high[:, which, k, :], start=(k == 0), stop=False)
                        nc.tensor.matmul(ps, hT_low[:, k, bs], thin_high[:, which, k, :], start=False, stop=False)
                        last = nc.tensor.matmul(ps, hT_high[:, k, bs], thin_low[:, which, k, :],
                                                start=False, stop=(k == KD - 1))
                last.then_inc(fill_done, 1)

            def modulation(mod_use, turns=0, more_uses=0):
                m, use = mod_use
                wait_free(pe, use, more_uses)
                wait_mod(pe, m, 8, turns)
                for f in range(4):
                    last = nc.tensor.matmul(pair(use)[:, f:f + 1], mod_total(m)[:, f * P:(f + 1) * P], ones_col,
                                            start=True, stop=True)
                last.then_inc(fill_done, 1)

            def down_product(c, high_in, low_in, first, last_one, turns=0):
                for j in range(2):
                    s = 2 * c + j
                    high, low = piece(w_high, s, 2, D), piece(w_low, s, 2, D)
                    wait_high(s, turns)
                    if last_one and j == 1:
                        wait_low(s, turns)
                        for b in range(TB):
                            bs = slice(b * P, (b + 1) * P)
                            for n in range(2):
                                y, ns = y_sum[:, b, n * 512:(n + 1) * 512], slice(n * 512, (n + 1) * 512)
                                for k in range(2):
                                    hi_in, lo_in = high_in[:, 2 + k, bs], low_in[:, 2 + k, bs]
                                    nc.tensor.matmul(y, hi_in, high[:, k, ns], start=False, stop=False)
                                    nc.tensor.matmul(y, lo_in, high[:, k, ns], start=False, stop=False)
                                    last = nc.tensor.matmul(y, hi_in, low[:, k, ns], start=False, stop=(k == 1))
                            last.then_inc(piece_done if b else first_block_done, 1)
                        continue
                    for b in range(TB):
                        for n in range(2):
                            y, ns = y_sum[:, b, n * 512:(n + 1) * 512], slice(n * 512, (n + 1) * 512)
                            for k in range(2):
                                kk = 2 * j + k
                                nc.tensor.matmul(y, high_in[:, kk, b * P:(b + 1) * P], high[:, k, ns],
                                                 start=(first and kk == 0), stop=False)
                                nc.tensor.matmul(y, low_in[:, kk, b * P:(b + 1) * P], high[:, k, ns],
                                                 start=False, stop=False)
                    wait_low(s, turns)
                    for b in range(TB):
                        for n in range(2):
                            y, ns = y_sum[:, b, n * 512:(n + 1) * 512], slice(n * 512, (n + 1) * 512)
                            for k in range(2):
                                kk = 2 * j + k
                                last = nc.tensor.matmul(y, high_in[:, kk, b * P:(b + 1) * P], low[:, k, ns],
                                                        start=False, stop=False)
                    last.then_inc(piece_done, 1)

            def transposes(use, src, k0, n=4, waits=None):
                ps = quads(pair(use)[:, :])
                wait_free(pe, use)
                for b in range(TB):
                    if waits is not None:
                        waits(b)
                    for k in range(n):
                        last = nc.tensor.transpose(ps[:, k, b * P:(b + 1) * P],
                                                   src[:, b, (k0 + k) * P:(k0 + k + 1) * P], ident)
                last.then_inc(fill_done, 1)

            def norm(n):
                def waits(b):
                    if n.late:
                        pe.wait_ge(updated, TB * (n.after - 1) + b + 1)
                    else:
                        pe.wait_ge(scaled, TB * n.scaled + b + 1)
                transposes(n.uses[0], x if n.late else xn, 0, waits=waits)
                transposes(n.uses[1], x if n.late else xn, 4)
                wait_emptied(pe, n.uses[1])

            def gate_rows(uses, layer):
                for use, at in zip(uses, (G1, G2)):
                    wait_free(pe, use)
                    for k in range(KD):
                        j = MOD[layer] + at + k
                        last = nc.tensor.matmul(pair(use)[:, k * P:(k + 1) * P],
                                                mod[:, j:j + 1].to_broadcast([P, P]), ident, start=True, stop=True)
                    last.then_inc(fill_done, 1)

            def attention(a, dh, q, k, v, qT, kT, o, dv, o_wait):
                if a.packed:
                    for j in range(2):
                        for use, src in zip(a.kq[2 * j:2 * j + 2], (q, k)):
                            transposes(use, tokpair(src), 4 * j)
                else:
                    for g in range(4):
                        for use, src in zip(a.kq[2 * g:2 * g + 2], (q, k)):
                            wait_free(pe, use)
                            ps = quads(pair(use)[:, :])
                            for b in range(TB):
                                for i in range(4):
                                    last = nc.tensor.transpose(ps[0:dh, i, b * P:(b + 1) * P],
                                                               heads_of(src, dh)[:, b, 4 * g + i, :], ident)
                            last.then_inc(fill_done, 1)
                for use in a.kq[-2:]:
                    wait_emptied(pe, use)

                def head(area, h):
                    if a.packed:
                        at = (h % 2) * HD
                        return area.rearrange("p (h t) -> p h t", t=S)[at:at + HD, h // 2, :]
                    return area.rearrange("p (h t) -> p h t", t=S)[0:dh, h, :]

                def scores(n):
                    g, qb = n // 2, n % 2
                    use = a.scores[n]
                    ps = quads(pair(use)[:, :])
                    wait_free(pe, use)
                    for i in range(4):
                        h = 4 * g + head_at(i)
                        last = nc.tensor.matmul(ps[:, i, 0:(qb + 1) * P], head(qT, h)[:, qb * P:(qb + 1) * P],
                                                head(kT, h)[:, 0:(qb + 1) * P], start=True, stop=True)
                    last.then_inc(fill_done, 1)

                def turn_round(n):
                    qb, at = n % 2, a.unit + n
                    pe.wait_ge(probs_ready, at + 1)
                    if at >= 1:
                        pe.wait_ge(pT_ready, at)
                    for i in range(4):
                        for kb in range(qb + 1):
                            last = nc.tensor.transpose(pT_ps[:, i, kb * P:(kb + 1) * P],
                                                       probs[:, n % 3, i, kb * P:(kb + 1) * P], ident)
                    last.then_inc(pT_done, 1)

                def weigh(n):
                    g, qb, at = n // 2, n % 2, a.unit + n
                    pe.wait_ge(pT_ready, at + 1)
                    if at >= 2:
                        pe.wait_ge(o_taken, at - 1)
                    for i in range(4):
                        h, at_o = 4 * g + head_at(i), head_at(i) * dv
                        v0 = (h * HD) if dv == HD else (h // 2) * dv
                        for kb in range(qb + 1):
                            last = nc.tensor.matmul(o_ps[n % 2][:, at_o:at_o + dv],
                                                    pT[:, n % 2, i, kb * P:(kb + 1) * P],
                                                    tokpair(v)[:, kb, v0:v0 + dv], start=(kb == 0), stop=(kb == qb))
                    last.then_inc(pv_done, 1)

                for n in range(3):
                    scores(n)
                for n in range(8):
                    turn_round(n)
                    if n + 3 < 8:
                        scores(n + 3)
                    weigh(n)
                o_wait()
                for j in range(2):
                    transposes(a.oT[j], tokpair(o), 4 * j)
                wait_emptied(pe, a.oT[1])
                for j in range(2):
                    down_product(a.wo[j], hT_high[:, 4 * j:4 * j + 4, :], hT_low[:, 4 * j:4 * j + 4, :], j == 0, j == 1)

            def attention_done(a):
                def wait():
                    pe.wait_ge(o_taken, a.unit + 8)
                return wait

            def experts(m):
                norm(m.norm)
                thin_product(m.router, 1)

                def down(e, t=0):
                    pe.wait_ge(gated_ready, t * 2 + (m.first + e + 1))
                    at = (m.first + e) % 2
                    down_product(m.down[e], gated_high[:, at], gated_low[:, at], e == 0, e == EXPERTS - 1, t)

                def one(e, t=0):
                    uses = t * TURN_USES[bool(m.mod)]
                    transposed_product(m.gate[e], t, uses)
                    transposed_product(m.up[e], t, uses)
                    if e:
                        down(e - 1, t)
                    if m.mod:
                        modulation(m.mod[e], t, uses)

                one(0)
                pe.wait_ge(combined, (1 if m is plan.moe0 else 2))
                for j, use in enumerate(m.comb):
                    wait_free(pe, use)
                    ps = quads(pair(use)[:, :])
                    for i in range(4):
                        for b in range(TB):
                            col = route[:, 9, b * EXPERTS + 4 * j + i:b * EXPERTS + 4 * j + i + 1]
                            last = nc.tensor.matmul(ps[:, i, b * P:(b + 1) * P],
                                                    col.to_broadcast([P, P]), ident, start=True, stop=True)
                    last.then_inc(fill_done, 1)
                one(1)
                with pe.Fori(0, TURNS) as t:
                    for i in range(2):
                        one(2 + i, t)
                down(EXPERTS - 1)

            def mlp(m):
                norm(m.norm)
                for j in range(FF_PARTS + 1):
                    if j < FF_PARTS:
                        transposed_product(m.up[j])
                    if j:
                        pe.wait_ge(gated_ready, m.first + j)
                        at = (m.first + j - 1) % 2
                        down_product(m.down[j - 1], gated_high[:, at], gated_low[:, at], j == 1, j == FF_PARTS)

            def retention(r):
                norm(r.norm)
                for c, use in enumerate(r.proj):
                    if c < 4:
                        transposed_product(use)
                    else:
                        token_product(use)
                wait_emptied(pe, r.proj[3])
                wait_emptied(pe, r.proj[7])

                def scores(h):
                    use = r.scores[h]
                    ps = pair(use)
                    wait_free(pe, use)
                    for half in range(2):
                        nc.tensor.matmul(ps[:, 0:S], r_kT[:, 2 * h + half, 0:P], r_qT[:, 2 * h + half, :],
                                         start=(half == 0), stop=(half == 1))
                    for half in range(2):
                        last = nc.tensor.matmul(ps[:, 512:512 + P], r_kT[:, 2 * h + half, P:S],
                                                r_qT[:, 2 * h + half, P:S], start=(half == 0), stop=(half == 1))
                    last.then_inc(fill_done, 1)

                def weigh(h):
                    wait_emptied(pe, r.scores[h])
                    if r.head + h >= 2:
                        pe.wait_ge(r_taken, r.head + h - 1)
                    o = tokpair(Y[:, (h % 2) * 1024:(h % 2 + 1) * 1024])
                    sT, vs = r_s[:, h % 2], slice(h * RDV, (h + 1) * RDV)
                    nc.tensor.matmul(o[:, 0, :], sT[:, 0:P], r_v[:, 0, vs], start=True, stop=True)
                    nc.tensor.matmul(o[:, 1, :], sT[:, P:S], r_v[:, 0, vs], start=True, stop=False)
                    nc.tensor.matmul(o[:, 1, :], sT[:, S:S + P], r_v[:, 1, vs],
                                     start=False, stop=True).then_inc(r_pv_done, 1)

                scores(0)
                for h in range(RH):
                    if h + 1 < RH:
                        scores(h + 1)
                    weigh(h)
                pe.wait_ge(r_taken, r.head + RH)
                for j in range(4):
                    transposes(r.oT[j], r_o, 4 * j)
                for j in range(4):
                    wait_emptied(pe, r.oT[j])
                    down_product(r.wo[j], *r_blocks(j), j == 0, j == 3)

            pe.wait_ge(rows_loaded, 16 * early)
            use = plan.columns
            nc.tensor.transpose(pair(use)[:, 0:P], rows[:, 0:P], ident)
            nc.tensor.transpose(pair(use)[:, P:2 * P], rows[:, P:2 * P], ident).then_inc(fill_done, 1)
            pe.wait_ge(const_loaded, 16 * N_CONST)
            nc.tensor.matmul(pair(plan.rel)[0:16, 0:S], rel_in, onehot, start=True, stop=True).then_inc(fill_done, 1)
            for use in plan.mod_a:
                modulation(use)
            norm(plan.a_norm)
            pe.wait_ge(thin_ready, 1)
            thin_product(plan.f_logit, 0)
            for j in range(6):
                token_product(plan.a_proj[j])
                use, ones_m = plan.cum[j], ones_col.to_broadcast([P, P])
                if j == 0:
                    pe.wait_ge(logf_ready, 1)
                    wait_free(pe, use)
                    nc.tensor.matmul(pair(use)[:, 0:HEADS], upto_m, logf[:, 0, :], start=True, stop=True)
                    nc.tensor.matmul(pair(use)[:, HEADS:2 * HEADS], ones_m, logf[:, 0, :], start=True, stop=False)
                    nc.tensor.matmul(pair(use)[:, HEADS:2 * HEADS], upto_m, logf[:, 1, :],
                                     start=False, stop=True).then_inc(fill_done, 1)
                elif j < 5:
                    wait_free(pe, use)
                    ps = quads(pair(use)[:, :])
                    for i in range(4):
                        h = 4 * (j - 1) + i
                        f0 = logf[:, 0, h:h + 1].to_broadcast([P, P])
                        f1 = logf[:, 1, h:h + 1].to_broadcast([P, P])
                        nc.tensor.matmul(ps[:, i, 0:P], f0, upto_m, start=True, stop=True)
                        nc.tensor.matmul(ps[:, i, P:S], f0, ones_m, start=True, stop=False)
                        last = nc.tensor.matmul(ps[:, i, P:S], f1, upto_m, start=False, stop=True)
                    last.then_inc(fill_done, 1)
                for use in plan.a_mods[j]:
                    modulation(use)
            wait_emptied(pe, plan.a_mods[5][-1][1])
            gate_rows(plan.gates_a, 0)
            wait_emptied(pe, plan.a_proj[5])
            attention(plan.att_a, HD, q_area, k_area, v_area, qT_area, kT_area, o_area, HD, attention_done(plan.att_a))
            experts(plan.moe0)
            norm(plan.kv_norm)
            token_product(plan.kv_down, KD, KV_RANK + ROPE)
            pe.wait_ge(latent_ready, 1)
            use = plan.ckvT
            wait_free(pe, use)
            for b in range(TB):
                for k in range(2):
                    last = nc.tensor.transpose(quads(pair(use)[:, :])[:, k, b * P:(b + 1) * P],
                                               ckv[:, b, k * P:(k + 1) * P], ident)
            last.then_inc(fill_done, 1)
            wait_emptied(pe, use)
            for use in plan.kv_up:
                token_product(use, 2)
            norm(plan.b_norm)
            token_product(plan.dq[0])
            token_product(plan.dq[1], KD, 256)
            pe.wait_ge(latent_ready, 2)
            transposes(plan.cqT[0], cq, 0)
            transposes(plan.cqT[1], cq, 4, 2)
            wait_emptied(pe, plan.cqT[1])
            for use in plan.uq:
                token_product(use, 6)
            gate_rows(plan.gates_b, 1)
            pe.wait_ge(qk_ready, 1)
            attention(plan.att_b, QK_B, b_q, b_k, b_v, b_qT, b_kT, b_o, HD, attention_done(plan.att_b))
            experts(plan.moe1)
            retention(plan.ret0)
            mlp(plan.mlp0)

            def softmax_layer(a, nth, mlp_plan_):
                norm(a.norm)
                for use in a.proj:
                    token_product(use)
                pe.wait_ge(qk_ready, nth)
                wait_emptied(pe, a.proj[5])
                if a.diff:
                    def o_wait():
                        pe.wait_ge(o_ready, 1)
                    dv = 2 * HD
                else:
                    o_wait, dv = attention_done(a.att), HD
                attention(a.att, HD, q_area, k_area, v_area, qT_area, kT_area, o_area, dv, o_wait)
                mlp(mlp_plan_)

            softmax_layer(plan.moba, 2, plan.mlp1)
            softmax_layer(plan.diff, 3, plan.mlp2)
            retention(plan.ret1)
            mlp(plan.mlp3)

        @block.scalar
        def _(se):
            links, fed = [0], [0]

            def link(ins):
                links[0] += 1
                ins.then_inc(achain, 1)
                se.wait_ge(achain, links[0])

            def high(s, turns=0):
                n = plan.sizes[s]
                wait_raw(se, s, turns)
                if s >= RING:
                    wait_piece(se, s - RING, turns)
                nc.scalar.activation(w_high[:, s % RING, 0:n], raw[:, s % RING, 0:n], ACT.Copy).then_inc(high_ready, 1)

            def feed(n):
                while fed[0] < min(n, len(plan.sizes)):
                    high(fed[0])
                    fed[0] += 1

            def squares_of(src, dst, stat, waits=None):
                for b in range(TB):
                    if waits is not None:
                        waits(b)
                    last = nc.scalar.activation(dst[b], src[b], ACT.Square, accum_out=ss[:, stat % 2, b:b + 1])
                last.then_inc(squared, 1)

            def norm_squares(n, scratch):
                def waits(b):
                    if n.after:
                        se.wait_ge(updated, TB * (n.after - 1) + b + 1)
                    else:
                        se.wait_ge(x_loaded, 16)
                squares_of([x[:, b, :] for b in range(TB)], [scratch[:, b, :] for b in range(TB)], n.stat, waits)

            def norm_high(n, g, shift=None, tmp=None):
                for j, use in enumerate(n.uses):
                    wait_full(se, use)
                    ps = quads(pair(use)[:, :])
                    for i in range(4):
                        k = 4 * j + i
                        if shift is None:
                            last = nc.scalar.activation(hT_high[:, k, :], ps[:, i, :], ACT.Identity, scale=g[:, k:k + 1])
                        else:
                            last = nc.scalar.activation(quads_of(tmp, j)[:, i, :], ps[:, i, :], ACT.Identity,
                                                        bias=mod[:, shift + k:shift + k + 1], scale=g[:, k:k + 1])
                    last.then_inc(hT_high_made, 1)

            def norm(n, g, shift=None, tmp=xn_tmp):
                if n.late:
                    norm_high(n, g, shift)
                    norm_squares(n, tokpair(qT_area))
                else:
                    if not n.again:
                        norm_squares(n, xn)
                    norm_high(n, g, shift, tmp)
                feed(n.feed)

            def copy_out(dst, use, src):
                wait_full(se, use)
                nc.scalar.activation(dst, src, ACT.Copy).then_inc(emptied[use.u % 2], 1)

            def copy_chunk(dst, use, src):
                feed(2 * use.chunk + 4)
                copy_out(dst, use, src)
                feed(2 * use.chunk + 5)

            def high_of(dst, use, n, g=None):
                wait_full(se, use)
                ps = quads(pair(use)[:, :])
                if g is None:
                    last = nc.scalar.activation(dst, ps, ACT.Copy)
                else:
                    for k in range(n):
                        last = nc.scalar.activation(dst[:, k, :], ps[:, k, :], ACT.Identity, scale=g[:, k:k + 1])
                last.then_inc(hT_high_made, 1)

            def attention(a, dh, qT, q_scale=None, o_scale=None):
                copy = ACT.Copy if q_scale is None else ACT.Identity
                more = {} if q_scale is None else {"scale": q_scale}
                for j, use in enumerate(a.kq[0::2]):
                    wait_full(se, use)
                    nc.scalar.activation(quads_of(qT, j)[0:dh], quads(pair(use)[:, :])[0:dh], copy,
                                         **more).then_inc(emptied[use.u % 2], 1)

                def exponentials(n):
                    nk = (n % 2 + 1) * P
                    se.wait_ge(max_ready, a.unit + n + 1)
                    for i in range(4):
                        p = probs[:, n % 3, i, 0:nk]
                        last = nc.scalar.activation(p, p, ACT.Exp, bias=negmax[:, n % 3, i:i + 1],
                                                    accum_out=expsum[:, n % 3, i:i + 1])
                    last.then_inc(probs_ready, 1)

                exponentials(0)
                exponentials(1)
                for n in range(8):
                    nk = (n % 2 + 1) * P
                    se.wait_ge(pT_done, a.unit + n + 1)
                    nc.scalar.activation(pT[:, n % 2, :, 0:nk], pT_ps[:, :, 0:nk], ACT.Copy).then_inc(pT_ready, 1)
                    if n + 2 < 8:
                        exponentials(n + 2)
                for j, use in enumerate(a.oT):
                    dst = hT_high[:, 4 * j:4 * j + 4, :]
                    wait_full(se, use)
                    src = quads(pair(use)[:, :])
                    if o_scale is None:
                        nc.scalar.activation(dst, src, ACT.Copy).then_inc(hT_high_made, 1)
                    else:
                        nc.scalar.activation(dst, src, ACT.Identity, scale=o_scale).then_inc(hT_high_made, 1)
                feed(2 * a.wo[0] + 5)
                feed(2 * a.wo[1] + 4)

            def experts(m, layer):
                norm(m.norm, gain, MOD[layer] + SH2)
                wait_full(se, m.router)
                nc.scalar.activation(route[:, 0, :], pair(m.router)[:, 0:TB * EXPERTS],
                                     ACT.Sigmoid).then_inc(emptied[m.router.u % 2], 1)

                def one(e, t=0):
                    use, s = m.gate[e], 2 * m.gate[e].chunk
                    high(s + 3, t)
                    wait_full(se, use, t)
                    nc.scalar.activation(act[:, (m.first + e) % 2], quads(pair(use)[:, :]),
                                         ACT.Silu).then_inc(emptied[use.u % 2], 1)
                    high(s + 4, t)
                    high(s + 5, t)
                    if e == 0:
                        high(s + 6)
                        for j, use in enumerate(m.comb):
                            copy_out(comb[:, 4 * j:4 * j + 4, :], use, quads(pair(use)[:, :]))
                    at = m.first + e
                    se.wait_ge(product_ready, t * 2 + (at + 1))
                    nc.scalar.activation(gated_high[:, at % 2], prod[:], ACT.Copy).then_inc(gated_high_made, 1)
                    if e:
                        for k in range(6, 9):
                            high(s + k, t)

                one(0)
                one(1)
                with se.Fori(0, TURNS) as t:
                    for i in range(2):
                        one(2 + i, t)
                fed[0] = 2 * m.down[-1] + 3
                feed(2 * m.down[-1] + 4)

            def mlp(m, layer):
                norm(m.norm, cols[:, N2_G + layer * KD:N2_G + (layer + 1) * KD])
                for j in range(FF_PARTS):
                    use, at = m.up[j], m.first + j
                    feed(2 * use.chunk + 4)
                    wait_full(se, use)
                    nc.scalar.activation(act[:, at % 2], quads(pair(use)[:, :]), ACT.Relu).then_inc(emptied[use.u % 2], 1)
                    feed(2 * use.chunk + 5)
                    se.wait_ge(product_ready, at + 1)
                    nc.scalar.activation(gated_high[:, at % 2], prod[:], ACT.Copy).then_inc(gated_high_made, 1)
                    if j:
                        feed(2 * m.down[j - 1] + 5)
                feed(2 * m.down[-1] + 4)

            def retention(r, layer):
                norm(r.norm, cols[:, N1_G + layer * KD:N1_G + (layer + 1) * KD])
                feed(2 * r.proj[3].chunk + 5)
                for c in range(4):
                    use = r.proj[4 + c]
                    copy_chunk(r_v[:, :, c * 512:(c + 1) * 512], use, tokpair(pair(use)[:, :]))
                for c in range(4):
                    use = r.proj[8 + c]
                    feed(2 * use.chunk + 4)
                    wait_full(se, use)
                    nc.scalar.activation(r_g[:, :, c * 512:(c + 1) * 512], tokpair(pair(use)[:, :]),
                                         ACT.Silu).then_inc(emptied[use.u % 2], 1)
                    feed(2 * use.chunk + 5)
                for h in range(RH):
                    se.wait_ge(r_pv_done, r.head + h + 1)
                    o = tokpair(Y[:, (h % 2) * 1024:(h % 2 + 1) * 1024])
                    squares_of([o[:, b, :] for b in range(TB)],
                               [r_o[:, b, h * RDV:(h + 1) * RDV] for b in range(TB)], r.stat[h])
                for j, use in enumerate(r.oT):
                    high_of(r_blocks(j)[0], use, 4)
                for c in r.wo[:-1]:
                    feed(2 * c + 5)
                feed(2 * r.wo[-1] + 4)

            for dst, src in small_loads[:early]:
                se.dma_start(dst, src, allow_slow_non_contiguous=True).then_inc(rows_loaded, 16)
            se.dma_start(x[:], w["x"][0].rearrange("(b p) n -> p b n", p=P)).then_inc(x_loaded, 16)
            wait_emptied(se, plan.columns)
            nc.scalar.activation(c_act[:], cols[:, C_IN:C_IN + KD], ACT.Silu).then_inc(c_ready, 1)
            norm_squares(plan.a_norm, y_sum)
            se.wait_ge(const_loaded, 16 * N_CONST)
            nc.scalar.activation(thin_high[:], thin, ACT.Copy).then_inc(thin_high_made, 1)
            feed(RING)
            norm_high(plan.a_norm, gain, MOD[0] + SH1, v_area)
            wait_emptied(se, plan.f_logit)
            link(nc.scalar.activation(logw[:], cumq[:], ACT.Abs))
            link(nc.scalar.activation(logw[:], logw[:], ACT.Exp, scale=-1.0))
            nc.scalar.activation(logw[:], logw[:], ACT.Ln, bias=1.0).then_inc(softplus_ready, 1)
            wait_emptied(se, plan.rel)
            se.dma_start(rel_scratch, spread(rel_rows, 1, P)).then_inc(rel_stored, 16)
            se.wait_ge(lam_ready, 1)
            nc.scalar.activation(lam[:, 2:4], lam[:, 0:2], ACT.Exp).then_inc(lam_ready, 1)
            se.wait_ge(turns_ready, 1)
            nc.scalar.activation(rope[:], ropew[:], ACT.Sin).then_inc(rope_ready, 1)

            def by_token(proj, between=None, kept=None):
                for j, use in enumerate(proj):
                    half, area = (j % 2) * 512, (q_area, k_area, v_area)[j // 2]
                    feed(2 * use.chunk + 4)
                    if between is not None and j == 2:
                        se.wait_ge(rel_stored, 16)
                    dst, src = tokpair(area)[:, :, half:half + 512], tokpair(pair(use)[:, :])
                    if kept is None:
                        copy_out(dst, use, src)
                    else:
                        se.wait_ge(kept_ready, kept + 1)
                        wait_full(se, use)
                        for b in range(TB):
                            last = nc.scalar.activation(dst[:, b, :], src[:, b, :], ACT.Identity,
                                                        scale=rs_kept[:, b:b + 1])
                        last.then_inc(emptied[use.u % 2], 1)
                    if between is not None:
                        between(j)
                    feed(2 * use.chunk + 5)

            def running_sums(j):
                use = plan.cum[j]
                if j == 0:
                    copy_out(cumq[:], use, pair(use)[:, 0:TB * HEADS].rearrange("p (b h) -> p b h", b=TB))
                    wait_emptied(se, use)
                elif j < 5:
                    wait_full(se, use)
                    ps = quads(pair(use)[:, :])
                    for i in range(4):
                        h, at = 4 * (j - 1) + i, 4 * (j - 1) + head_at(i)
                        nc.scalar.activation(bias0[:, at, :], ps[:, i, 0:P], ACT.Identity,
                                             bias=cumq[:, 0, h:h + 1], scale=-1.0)
                        last = nc.scalar.activation(bias1[:, at, :], ps[:, i, :], ACT.Identity,
                                                    bias=cumq[:, 1, h:h + 1], scale=-1.0)
                    last.then_inc(emptied[use.u % 2], 1)

            by_token(plan.a_proj, running_sums)
            for i, use in enumerate(plan.gates_a):
                copy_out(gates[:, i, :], use, pair(use)[:, :])
            attention(plan.att_a, P, qT_area)
            experts(plan.moe0, 0)
            norm(plan.kv_norm, gain, MOD["kv"])
            use = plan.kv_down
            copy_chunk(ckv, use, tokpair(pair(use)[:, :])[:, :, 0:KV_RANK + ROPE])
            wait_emptied(se, use)
            squares_of([ckv[:, b, 0:KV_RANK] for b in range(TB)],
                       [tokpair(b_tmp)[:, b, 0:KV_RANK] for b in range(TB)], plan.kv_stat)
            high_of(hT_high[:, 0:2, :], plan.ckvT, 2, cols[:, LAT_G:LAT_G + 2])
            for j, use in enumerate(plan.kv_up):
                feed(2 * use.chunk + 4)
                wait_full(se, use)
                ps = pair(use)[:, :].rearrange("p (b h n) -> p b h n", b=TB, h=4)
                kv = heads_of(b_k, QK_B)[:, :, 4 * j:4 * j + 4, 0:NOPE]
                vv = heads_of(b_v)[:, :, 4 * j:4 * j + 4, :]
                for b in range(TB):
                    nc.scalar.activation(kv[:, b], ps[:, b, :, 0:NOPE], ACT.Copy)
                    last = nc.scalar.activation(vv[:, b], ps[:, b, :, NOPE:2 * NOPE], ACT.Copy)
                last.then_inc(emptied[use.u % 2], 1)
                feed(2 * use.chunk + 5)
            norm(plan.b_norm, gain_b, MOD[1] + SH1, b_tmp)
            copy_chunk(cq[:, :, 0:512], plan.dq[0], tokpair(pair(plan.dq[0])[:, :]))
            copy_chunk(cq[:, :, 512:768], plan.dq[1], tokpair(pair(plan.dq[1])[:, :])[:, :, 0:256])
            wait_emptied(se, plan.dq[0])
            wait_emptied(se, plan.dq[1])
            squares_of([cq[:, b, :] for b in range(TB)],
                       [tokpair(b_tmp)[:, b, 0:Q_RANK] for b in range(TB)], plan.cq_stat)
            high_of(hT_high[:, 0:4, :], plan.cqT[0], 4, cols[:, BQ_G:BQ_G + 4])
            high_of(hT_high[:, 4:6, :], plan.cqT[1], 2, cols[:, BQ_G + 4:BQ_G + 6])
            for j, use in enumerate(plan.uq):
                copy_chunk(tokpair(b_q)[:, :, j * 512:(j + 1) * 512], use, tokpair(pair(use)[:, :]))
            for i, use in enumerate(plan.gates_b):
                copy_out(gates[:, i, :], use, pair(use)[:, :])
            attention(plan.att_b, QK_B, b_qT)
            se.wait_ge(updated, TB * (plan.att_b.update + 1))
            se.dma_start(final_gain, w["final_norm_g"].unsqueeze(0).to_broadcast([P, D])).then_inc(gain_loaded, 16)
            experts(plan.moe1, 1)
            squares_of([x[:, b, :] for b in range(TB)], [xn[:, b, :] for b in range(TB)], plan.final_stat,
                       lambda b: se.wait_ge(updated, TB * plan.moe1.update + b + 1))
            retention(plan.ret0, 0)
            wait_piece(se, 2 * plan.ret0.wo[0])
            se.wait_ge(rel_stored, 16)
            rows_at = bass.AP(rel_scratch.tensor, P - 1, [[383, P], [384 * P, HEADS], [1, S]])
            se.dma_start(relbias, rows_at).then_inc(rel_loaded, 16)
            mlp(plan.mlp0, 0)

            def softmax_layer(a, nth, layer):
                norm(a.norm, cols[:, N1_G + layer * KD:N1_G + (layer + 1) * KD])
                by_token(a.proj, kept=a.norm.kept)
                attention(a.att, P, qT_area, head_gain[:, 2 * nth:2 * nth + 1], subln[:, 0:1] if a.diff else None)

            softmax_layer(plan.moba, 0, 1)
            mlp(plan.mlp1, 1)
            softmax_layer(plan.diff, 1, 2)
            mlp(plan.mlp2, 2)
            retention(plan.ret1, 3)
            mlp(plan.mlp3, 3)

        @block.vector
        def _(ve):
            links, fed, sums = [0], [0], [0]
            V = nc.vector

            def link(ins):
                links[0] += 1
                ins.then_inc(vchain, 1)
                ve.wait_ge(vchain, links[0])

            def empties(use, ins):
                ins.then_inc(emptied[use.u % 2], 1)

            def low(s, turns=0):
                n = plan.sizes[s]
                ve.wait_ge(high_ready, turns * TURN_PIECES + (s + 1))
                V.tensor_tensor(w_low[:, s % RING, 0:n], raw[:, s % RING, 0:n],
                                w_high[:, s % RING, 0:n].bitcast(F32), ALU.subtract).then_inc(low_ready, 1)

            def feed(n):
                while fed[0] < min(n, len(plan.sizes)):
                    low(fed[0])
                    fed[0] += 1

            def mod_rows(m, k0, k1, turns=0):
                total = mod_total(m)
                for k in range(k0, k1):
                    h = k // 4
                    if m < FIRST_MODS:
                        part = first_raw[:, 2 * m + h, k % 4]
                        if k % 4 == 0:
                            ve.wait_ge(first_loaded[2 * m + h], 16)
                    else:
                        part = mod_raw[:, h, k % 4]
                        if k % 4 == 0:
                            ve.wait_ge(mod_loaded[h], turns * 32 + 16 * (m - FIRST_MODS + 1))
                    if k == 0:
                        V.tensor_scalar(total, part, c_act[:, 0:1], None, ALU.mult).then_inc(mod_step, 1)
                    else:
                        wait_mod(ve, m, k, turns)
                        V.scalar_tensor_tensor(total, part, c_act[:, k:k + 1], total,
                                               ALU.mult, ALU.add).then_inc(mod_step, 1)

            def mod_cols(mod_use, turns=0):
                m, use = mod_use
                wait_full(ve, use, turns)
                if isinstance(turns, int):
                    dst, bias = mod[:, 4 * m:4 * m + 4], cols[:, MOD_B + 4 * m:MOD_B + 4 * m + 4]
                else:
                    dst = mod[:, bass.ds(turns * 8 + 4 * m, 4)]
                    bias = cols[:, bass.ds(turns * 8 + (MOD_B + 4 * m), 4)]
                empties(use, V.tensor_tensor(dst, pair(use)[:, 0:4], bias, ALU.add))

            def gain_of(g, scale, out=gain):
                link(V.scalar_tensor_tensor(out[:], mod[:, scale:scale + KD], 1.0, cols[:, g:g + KD],
                                            ALU.add, ALU.mult))

            def low_of(dst_low, dst_high, use, index, n, g=None):
                ve.wait_ge(hT_high_made, index + 1)
                ps = quads(pair(use)[:, :])
                if g is None:
                    last = V.tensor_tensor(dst_low, ps, dst_high.bitcast(F32), ALU.subtract)
                else:
                    for k in range(n):
                        gk = g if g.shape[1] == 1 else g[:, k:k + 1]
                        last = V.scalar_tensor_tensor(dst_low[:, k, :], ps[:, k, :], gk,
                                                      dst_high[:, k, :].bitcast(F32), ALU.mult, ALU.subtract)
                empties(use, last)

            def norm(n, g, shift=None, tmp=None):
                if not n.late and not n.again:
                    ve.wait_ge(rs_ready, n.stat + 1)
                    for b in range(TB):
                        V.tensor_scalar(xn[:, b, :], x[:, b, :], rs[:, n.stat % 2, b:b + 1], None,
                                        ALU.mult).then_inc(scaled, 1)
                if not n.after:
                    feed(n.feed)
                tmp = xn_tmp if tmp is None else tmp
                for j, use in enumerate(n.uses):
                    ks = slice(4 * j, 4 * j + 4)
                    if shift is None:
                        low_of(hT_low[:, ks, :], hT_high[:, ks, :], use, n.high + j, 4, g[:, ks])
                        continue
                    ve.wait_ge(hT_high_made, n.high + j + 1)
                    t = quads_of(tmp, j)
                    link(V.tensor_copy(hT_high[:, ks, :], t))
                    empties(use, V.tensor_tensor(hT_low[:, ks, :], t, hT_high[:, ks, :].bitcast(F32), ALU.subtract))
                feed(n.feed)

            def keep(n, squared_too=False):
                ve.wait_ge(rs_ready, n.stat + 1)
                r = rs[:, n.stat % 2, 0:TB]
                if squared_too:
                    V.tensor_tensor(rs_kept[:], r, r, ALU.mult).then_inc(kept_ready, 1)
                else:
                    V.tensor_copy(rs_kept[:], r).then_inc(kept_ready, 1)

            def update(last_chunk, gate=None, kept=None):
                feed(2 * last_chunk + 4)
                sums[0] += 1
                ve.wait_ge(first_block_done, sums[0])
                if kept is not None:
                    ve.wait_ge(kept_ready, kept + 1)
                for b in range(TB):
                    if b:
                        wait_piece(ve, 2 * last_chunk + 1)
                    if kept is not None:
                        V.scalar_tensor_tensor(x[:, b, :], y_sum[:, b, :], rs_kept[:, b:b + 1], x[:, b, :],
                                               ALU.mult, ALU.add).then_inc(updated, 1)
                    elif gate is None:
                        V.tensor_tensor(x[:, b, :], x[:, b, :], y_sum[:, b, :], ALU.add).then_inc(updated, 1)
                    else:
                        link(V.tensor_tensor(xn[:, b, :], gates[:, gate, :], y_sum[:, b, :], ALU.mult))
                        V.tensor_tensor(x[:, b, :], x[:, b, :], xn[:, b, :], ALU.add).then_inc(updated, 1)

            def attention(a, dh, kT, o, scale, bias, k_scale=None, diff=False, o_stat=None):
                for j, use in enumerate(a.kq[1::2]):
                    wait_full(ve, use)
                    src, dst = quads(pair(use)[:, :])[0:dh], quads_of(kT, j)[0:dh]
                    if k_scale is None:
                        empties(use, V.tensor_copy(dst, src))
                    else:
                        empties(use, V.tensor_scalar(dst, src, k_scale, None, ALU.mult))

                def start(n):
                    g, nk, use = n // 2, (n % 2 + 1) * P, a.scores[n]
                    wait_full(ve, use)
                    s = probs[:, n % 3, :, 0:nk]
                    empties(use, V.scalar_tensor_tensor(s, quads(pair(use)[:, :])[:, :, 0:nk], scale,
                                                        bias(g, n % 2), ALU.mult, ALU.add))
                    wait_emptied(ve, use)
                    V.tensor_reduce(negmax[:, n % 3, :], s, X, ALU.max, negate=True).then_inc(max_ready, 1)

                def finish(n):
                    g, qb = n // 2, n % 2
                    ve.wait_ge(pv_done, a.unit + n + 1)
                    link(V.reciprocal(recip[:, n % 2, :].rearrange("p (i j) -> p i j", i=2),
                                      expsum[:, n % 3, :].rearrange("p (j i) -> p i j", i=2)))
                    dv = 2 * HD if diff else HD
                    heads = o_ps[n % 2][:, 0:4 * dv].rearrange("p (h d) -> p h d", h=4)
                    r = spread(recip[:, n % 2, :], 2, dv)
                    o_g = tokpair(o)[:, qb, g * 256:(g + 1) * 256]
                    if not diff:
                        V.tensor_tensor(o_g.rearrange("p (h d) -> p h d", h=4), heads, r, ALU.mult).then_inc(o_taken, 1)
                        return
                    V.tensor_tensor(diff_tmp.rearrange("p j i d -> p (j i) d"), heads, r, ALU.mult).then_inc(o_taken, 1)
                    ve.wait_ge(o_taken, a.unit + n + 1)
                    link(V.scalar_tensor_tensor(o_g.rearrange("p (j d) -> p j d", j=2),
                                                diff_tmp[:, :, 1, :], lam[:, 5:6], diff_tmp[:, :, 0, :],
                                                ALU.mult, ALU.add))

                start(0)
                start(1)
                for n in range(8):
                    if n + 2 < 8:
                        start(n + 2)
                    finish(n)
                if diff:
                    sq, oh = work[:, 0:2048], o.rearrange("p (h d) -> p h d", d=2 * HD)
                    link(V.tensor_tensor(sq, o, o, ALU.mult))
                    V.tensor_reduce(ss[:, o_stat % 2, 0:16], sq.rearrange("p (h d) -> p h d", d=2 * HD), X,
                                    ALU.add).then_inc(squared, 1)
                    ve.wait_ge(rs_ready, o_stat + 1)
                    V.tensor_tensor(oh, oh, spread(rs[:, o_stat % 2, 0:16], 2, 2 * HD), ALU.mult).then_inc(o_ready, 1)
                for j, use in enumerate(a.oT):
                    ks = slice(4 * j, 4 * j + 4)
                    low_of(hT_low[:, ks, :], hT_high[:, ks, :], use, a.high + j, 4, subln[:, 0:1] if diff else None)
                feed(2 * a.wo[0] + 5)

            def routing(nth):
                R = [route[:, k, :] for k in range(10)]
                sc, sel = R[0], R[1]
                G8 = TB * GROUPS

                def fours(ap):
                    return ap.rearrange("p (g e) -> p g e", e=4)

                link(V.tensor_tensor(sel.rearrange("p (b e) -> p b e", b=TB), sc.rearrange("p (b e) -> p b e", b=TB),
                                     spread(r_bias[:, :], 1, TB), ALU.add))
                s4 = sel.rearrange("p (g i j) -> p g i j", g=G8, i=2)
                hi, lo = R[2][:, 0:16], R[2][:, 16:32]
                hi2, lo2 = hi.rearrange("p (g i) -> p g i", i=2), lo.rearrange("p (g i) -> p g i", i=2)
                link(V.tensor_tensor(hi2, s4[:, :, :, 0], s4[:, :, :, 1], ALU.max))
                link(V.tensor_tensor(lo2, s4[:, :, :, 0], s4[:, :, :, 1], ALU.min))
                top1, mid, low, top2 = (R[3][:, 8 * k:8 * k + 8] for k in range(4))
                link(V.tensor_tensor(top1, hi2[:, :, 0], hi2[:, :, 1], ALU.max))
                link(V.tensor_tensor(mid, hi2[:, :, 0], hi2[:, :, 1], ALU.min))
                link(V.tensor_tensor(low, lo2[:, :, 0], lo2[:, :, 1], ALU.max))
                link(V.tensor_tensor(top2, mid, low, ALU.max))
                gs, best, mark = R[4][:, 0:8], R[4][:, 8:10], R[4][:, 16:24]
                first, here = R[4][:, 10:12], R[4][:, 24:32]

                def by_block(ap):
                    return ap.rearrange("p (b g) -> p b g", b=TB)

                link(V.tensor_tensor(gs, top1, top2, ALU.add))
                link(V.tensor_reduce(best, by_block(gs), X, ALU.max))
                link(V.tensor_tensor(by_block(mark), by_block(gs), spread(best, 2, GROUPS), ALU.is_ge))
                link(V.tensor_tensor(by_block(mark), by_block(mark), spread(descending, 1, TB), ALU.mult))
                link(V.tensor_reduce(first, by_block(mark), X, ALU.max))
                link(V.tensor_tensor(by_block(here), by_block(mark), spread(first, 2, GROUPS), ALU.is_equal))
                m1, m2 = R[5][:, 0:8], R[5][:, 8:16]
                link(V.tensor_tensor(fours(R[6]), fours(sel), spread(top1, 2, 4), ALU.is_ge))
                link(V.tensor_tensor(fours(R[6]), fours(R[6]), spread(descending, 1, G8), ALU.mult))
                link(V.tensor_reduce(m1, fours(R[6]), X, ALU.max))
                link(V.tensor_tensor(fours(R[6]), fours(R[6]), spread(m1, 2, 4), ALU.is_equal))
                link(V.scalar_tensor_tensor(R[7], R[6], NEG, sel, ALU.mult, ALU.add))
                link(V.tensor_reduce(m2, fours(R[7]), X, ALU.max))
                link(V.tensor_tensor(fours(R[8]), fours(R[7]), spread(m2, 2, 4), ALU.is_ge))
                link(V.tensor_tensor(fours(R[8]), fours(R[8]), spread(descending, 1, G8), ALU.mult))
                link(V.tensor_reduce(m1, fours(R[8]), X, ALU.max))
                link(V.tensor_tensor(fours(R[8]), fours(R[8]), spread(m1, 2, 4), ALU.is_equal))
                link(V.tensor_tensor(R[6], R[6], R[8], ALU.add))
                link(V.tensor_tensor(fours(R[6]), fours(R[6]), spread(here, 2, 4), ALU.mult))
                link(V.tensor_tensor(R[6], R[6], sc, ALU.mult))
                link(V.tensor_reduce(R[5][:, 16:18], R[6].rearrange("p (b e) -> p b e", b=TB), X, ALU.add))
                link(V.reciprocal(R[5][:, 18:20], R[5][:, 16:18]))
                V.tensor_tensor(R[9].rearrange("p (b e) -> p b e", b=TB), R[6].rearrange("p (b e) -> p b e", b=TB),
                                spread(R[5][:, 18:20], 2, EXPERTS), ALU.mult).then_inc(combined, 1)

            def gated_low_of(at, turns=0):
                ve.wait_ge(gated_high_made, turns * 2 + (at + 1))
                V.tensor_tensor(gated_low[:, at % 2], prod[:], gated_high[:, at % 2].bitcast(F32),
                                ALU.subtract).then_inc(gated_ready, 1)

            def experts(m, nth, layer):
                if m.mod:
                    wait_emptied(ve, plan.a_mods[5][-1][1])
                gain_of(FFN_G + layer * KD, MOD[layer] + SC2)
                norm(m.norm, gain, MOD[layer] + SH2)
                wait_emptied(ve, m.router)
                routing(nth)

                def one(e, t=0):
                    up, at, s = m.up[e], m.first + e, 2 * m.gate[e].chunk
                    uses = t * TURN_USES[bool(m.mod)]
                    low(s + 3, t)
                    if m.mod:
                        mod_rows(m.mod[e][0], 0, 4, t)
                    low(s + 4, t)
                    if m.mod:
                        mod_rows(m.mod[e][0], 4, 8, t)
                    low(s + 5, t)
                    if at:
                        ve.wait_ge(gated_ready, t * 2 + at)
                    wait_emptied(ve, m.gate[e], uses)
                    wait_full(ve, up, t)
                    empties(up, V.tensor_tensor(prod, act[:, at % 2], quads(pair(up)[:, :]), ALU.mult))
                    wait_emptied(ve, up, uses)
                    if e == 0:
                        low(s + 6)
                        if m.mod:
                            mod_cols(m.mod[e])
                        for use in m.comb:
                            wait_emptied(ve, use)
                    row = comb[:, e, :] if isinstance(t, int) else comb[:, bass.ds(t * 2 + e, 1), :].rearrange(
                        "p a t -> p (a t)")
                    V.tensor_tensor(prod, prod, spread(row, 1, 4), ALU.mult).then_inc(product_ready, 1)
                    ve.wait_ge(product_ready, t * 2 + (at + 1))
                    gated_low_of(at, t)
                    if e:
                        for k in range(6, 9):
                            low(s + k, t)
                        if m.mod:
                            mod_cols(m.mod[e], t)

                one(0)
                one(1)
                with ve.Fori(0, TURNS) as t:
                    for i in range(2):
                        one(2 + i, t)
                fed[0] = 2 * m.down[-1] + 3
                update(m.down[-1], 1)

            def mlp(m, layer):
                norm(m.norm, cols[:, N2_G + layer * KD:N2_G + (layer + 1) * KD])
                keep(m.norm, squared_too=True)
                for j in range(FF_PARTS):
                    use, at = m.up[j], m.first + j
                    feed(2 * use.chunk + 4)
                    wait_emptied(ve, use)
                    ve.wait_ge(gated_ready, at)
                    V.tensor_tensor(prod, act[:, at % 2], act[:, at % 2], ALU.mult).then_inc(product_ready, 1)
                    ve.wait_ge(product_ready, at + 1)
                    gated_low_of(at)
                    feed(2 * use.chunk + 5)
                    if j:
                        feed(2 * m.down[j - 1] + 5)
                update(m.down[-1], kept=m.norm.kept)

            def rotate(dst, use, c):
                wait_full(ve, use)
                ps = pair(use)[:, :].rearrange("p (h i t) -> p h i t", h=2, i=2)
                cos, sin = spread(rotary[:, 0, :], 1, 2), spread(rotary[:, 1, :], 1, 2)
                d = dst[:, 4 * c:4 * c + 4, :].rearrange("p (h i) t -> p h i t", i=2)
                V.tensor_tensor(r_tmp[:, 0], cos, ps[:, :, 0, :], ALU.mult)
                link(V.tensor_tensor(r_tmp[:, 1], sin, ps[:, :, 1, :], ALU.mult))
                link(V.tensor_tensor(d[:, :, 0, :], r_tmp[:, 0], r_tmp[:, 1], ALU.subtract))
                V.tensor_tensor(r_tmp[:, 0], sin, ps[:, :, 0, :], ALU.mult)
                link(V.tensor_tensor(r_tmp[:, 1], cos, ps[:, :, 1, :], ALU.mult))
                empties(use, V.tensor_tensor(d[:, :, 1, :], r_tmp[:, 0], r_tmp[:, 1], ALU.add))
                wait_emptied(ve, use)

            def retention(r, layer):
                norm(r.norm, cols[:, N1_G + layer * KD:N1_G + (layer + 1) * KD])
                for c in range(4):
                    feed(2 * r.proj[c].chunk + 4)
                    rotate((r_qT, r_kT)[c // 2], r.proj[c], c % 2)
                    feed(2 * r.proj[c].chunk + 5)
                feed(2 * r.proj[11].chunk + 5)

                def start(h):
                    use = r.scores[h]
                    wait_full(ve, use)
                    sT = r_s[:, h % 2]
                    V.tensor_tensor(sT[:, 0:S], decay[:, h, :], pair(use)[:, 0:S], ALU.mult)
                    empties(use, V.tensor_tensor(sT[:, S:S + P], decay[:, h, 0:P], pair(use)[:, 512:512 + P], ALU.mult))

                def finish(h):
                    ve.wait_ge(rs_ready, r.stat[h] + 1)
                    if h == 0:
                        wait_emptied(ve, r.proj[11])
                    o = tokpair(Y[:, (h % 2) * 1024:(h % 2 + 1) * 1024])
                    vs = slice(h * RDV, (h + 1) * RDV)
                    for b in range(TB):
                        last = V.scalar_tensor_tensor(r_o[:, b, vs], o[:, b, :], rs[:, r.stat[h] % 2, b:b + 1],
                                                      r_g[:, b, vs], ALU.mult, ALU.mult)
                    last.then_inc(r_taken, 1)

                ve.wait_ge(decay_loaded, 16 if r is plan.ret0 else 32)
                start(0)
                for h in range(RH):
                    if h + 1 < RH:
                        start(h + 1)
                    finish(h)
                for j, use in enumerate(r.oT):
                    high_part, low_part = r_blocks(j)
                    low_of(low_part, high_part, use, r.high + j, 4)
                for c in r.wo[:-1]:
                    feed(2 * c + 5)
                update(r.wo[3])

            wait_full(ve, plan.columns)
            empties(plan.columns, V.tensor_copy(cols[:], pair(plan.columns)[:, 0:2 * P]))
            ve.wait_ge(c_ready, 1)
            for m in range(FIRST_MODS):
                mod_rows(m, 0, 8)
            ve.wait_ge(const_loaded, 16 * N_CONST)
            V.memset(rel_rows[:, S:384], NEG)
            wait_full(ve, plan.rel)
            empties(plan.rel, V.tensor_copy(rel_rows[:, 0:S], pair(plan.rel)[0:16, 0:S]))
            ve.wait_ge(thin_high_made, 1)
            V.tensor_tensor(thin_low[:], thin, thin_high[:].bitcast(F32), ALU.subtract).then_inc(thin_ready, 1)
            for use in plan.mod_a:
                mod_cols(use)
            wait_emptied(ve, plan.mod_a[-1][1])
            gain_of(A_G, SC1)
            norm(plan.a_norm, gain, SH1, v_area)
            wait_full(ve, plan.f_logit)
            empties(plan.f_logit, V.tensor_tensor(
                cumq[:], spread(b_f[:, :], 1, TB),
                pair(plan.f_logit)[:, 0:TB * HEADS].rearrange("p (b h) -> p b h", b=TB), ALU.add))
            ve.wait_ge(softplus_ready, 1)
            V.scalar_tensor_tensor(logf[:], cumq[:], 0.0, logw[:], ALU.min, ALU.subtract).then_inc(logf_ready, 1)
            V.tensor_scalar(subln[:], subln[:], 1.0 - LAMBDA_INIT, None, ALU.mult)
            l4 = lam_in.rearrange("p (i j d) -> p i j d", i=2, j=2)
            link(V.tensor_tensor(lam_prod.rearrange("p (i d) -> p i d", i=2), l4[:, :, 0, :], l4[:, :, 1, :], ALU.mult))
            V.tensor_reduce(lam[:, 0:2], lam_prod.rearrange("p (i d) -> p i d", i=2), X, ALU.add).then_inc(lam_ready, 1)
            ve.wait_ge(lam_ready, 2)
            link(V.tensor_tensor(lam[:, 4:5], lam[:, 3:4], lam[:, 2:3], ALU.subtract))
            link(V.tensor_scalar(lam[:, 5:6], lam[:, 4:5], LAMBDA_INIT, None, ALU.subtract))
            link(V.tensor_copy(pos_f[:], pos_i[:]))
            for b in range(TB):
                link(V.tensor_scalar(ropew[:, 0, b, :], inv_rope, pos_f[:, b:b + 1], None, ALU.mult))
            link(V.tensor_copy(ropew[:, 1], ropew[:, 0]))
            TURN = 2.0 * np.pi
            ROUND = 1.5 * 2.0 ** 23
            link(V.tensor_scalar(rope[:, 0], ropew[:, 0], 1.0 / TURN, None, ALU.mult))
            link(V.tensor_scalar(rope[:, 1], ropew[:, 0], 1.0 / TURN, 0.25, ALU.mult, ALU.add))
            link(V.tensor_scalar(rope[:], rope[:], ROUND, None, ALU.add))
            link(V.tensor_scalar(rope[:], rope[:], ROUND, None, ALU.subtract))
            C1 = 6.28125
            C2 = float(np.float32(np.round((TURN - C1) * 2 ** 22) / 2 ** 22))
            C3 = float(np.float32(TURN - C1 - C2))
            for part in (C1, C2, C3):
                link(V.scalar_tensor_tensor(ropew[:], rope[:], -part, ropew[:], ALU.mult, ALU.add))
            link(V.tensor_scalar(ropew[:, 1], ropew[:, 1], float(np.pi / 2), None, ALU.add))
            V.tensor_scalar(ropew[:], ropew[:], 3.1415925, -3.1415925, ALU.min, ALU.max).then_inc(turns_ready, 1)
            m = FIRST_MODS
            mod_uses = dict(sum(plan.a_mods, []))
            for j in range(6):
                c = plan.a_proj[j].chunk
                feed(2 * c + 4)
                for _ in range((1, 1, 2, 1, 2, 1)[j]):
                    if m >= FIRST_MODS + 4:
                        wait_full(ve, mod_uses[m - 4])
                    mod_rows(m, 0, 8)
                    m += 1
                feed(2 * c + 5)
                for use in plan.a_mods[j]:
                    mod_cols(use)

            ve.wait_ge(masked, TB)
            attention(plan.att_a, P, kT_area, o_area, HD ** -0.5,
                      lambda g, qb: (bias0, bias1)[qb][:, 4 * g:4 * g + 4, :])
            update(plan.att_a.wo[1], 0)
            experts(plan.moe0, 1, 0)
            wait_emptied(ve, plan.moe0.mod[-1][1])
            gain_of(KV_G, MOD["kv"] + KD)
            gain_of(B_G, MOD[1] + SC1, gain_b)
            norm(plan.kv_norm, gain, MOD["kv"])
            feed(2 * plan.kv_down.chunk + 5)
            ve.wait_ge(rs_ready, plan.kv_stat + 1)
            ve.wait_ge(rope_ready, 1)
            for b in range(TB):
                last = V.tensor_scalar(ckv[:, b, 0:KV_RANK], ckv[:, b, 0:KV_RANK],
                                       rs[:, plan.kv_stat % 2, b:b + 1], None, ALU.mult)
            last.then_inc(latent_ready, 1)
            low_of(hT_low[:, 0:2, :], hT_high[:, 0:2, :], plan.ckvT, plan.ckv_high, 2, cols[:, LAT_G:LAT_G + 2])

            def rope_of(x1, x2, y1, y2, n):
                sin = spread(rope[:, 0], 2, n)
                cos = spread(rope[:, 1], 2, n)
                r4 = [rot[:, i, 0:TB * n * 16].rearrange("p (b h d) -> p b h d", b=TB, h=n) for i in range(4)]
                link(V.tensor_tensor(r4[0], x1, cos, ALU.mult))
                link(V.tensor_tensor(r4[1], x2, sin, ALU.mult))
                link(V.tensor_tensor(r4[2], x2, cos, ALU.mult))
                link(V.tensor_tensor(r4[3], x1, sin, ALU.mult))
                link(V.tensor_tensor(y1, r4[0], r4[1], ALU.subtract))
                return V.tensor_tensor(y2, r4[2], r4[3], ALU.add)

            kr = ckv[:, :, KV_RANK:KV_RANK + ROPE].unsqueeze(2)
            link(rope_of(kr[:, :, :, 0:16], kr[:, :, :, 16:32], kr[:, :, :, 0:16], kr[:, :, :, 16:32], 1))
            k4 = heads_of(b_k, QK_B)
            for b in range(TB):
                link(V.tensor_copy(k4[:, b, :, NOPE:QK_B], spread(ckv[:, b, KV_RANK:KV_RANK + ROPE], 1, HEADS)))
            feed(2 * plan.kv_up[-1].chunk + 5)
            norm(plan.b_norm, gain_b, MOD[1] + SH1, b_tmp)
            feed(2 * plan.dq[1].chunk + 5)
            ve.wait_ge(rs_ready, plan.cq_stat + 1)
            for b in range(TB):
                last = V.tensor_scalar(cq[:, b, :], cq[:, b, :], rs[:, plan.cq_stat % 2, b:b + 1], None, ALU.mult)
            last.then_inc(latent_ready, 1)
            low_of(hT_low[:, 0:4, :], hT_high[:, 0:4, :], plan.cqT[0], plan.cq_high, 4, cols[:, BQ_G:BQ_G + 4])
            low_of(hT_low[:, 4:6, :], hT_high[:, 4:6, :], plan.cqT[1], plan.cq_high + 1, 2,
                   cols[:, BQ_G + 4:BQ_G + 6])
            feed(2 * plan.uq[-1].chunk + 5)
            for use in plan.uq:
                wait_emptied(ve, use)
            q4 = heads_of(b_q, QK_B)
            q1, q2 = q4[:, :, :, NOPE:NOPE + 16], q4[:, :, :, NOPE + 16:QK_B]
            rope_of(q1, q2, q1, q2, HEADS).then_inc(qk_ready, 1)
            attention(plan.att_b, QK_B, b_kT, b_o, QK_B ** -0.5,
                      lambda g, qb: spread(chunked[:, P:S] if qb == 0 else chunked, 1, 4))
            update(plan.att_b.wo[1], 0)
            experts(plan.moe1, 2, 1)
            ve.wait_ge(rs_ready, plan.final_stat + 1)
            ve.wait_ge(gain_loaded, 16)
            for b in range(TB):
                V.scalar_tensor_tensor(x[:, b, :], x[:, b, :], rs[:, plan.final_stat % 2, b:b + 1], final_gain,
                                       ALU.mult, ALU.mult).then_inc(updated, 1)
            retention(plan.ret0, 0)
            mlp(plan.mlp0, 0)

            def softmax_layer(a, nth, layer):
                norm(a.norm, cols[:, N1_G + layer * KD:N1_G + (layer + 1) * KD])
                keep(a.norm)
                sq = o_area
                for i, area in enumerate((q_area, k_area)):
                    feed(2 * a.proj[2 * i + 1].chunk + 5)
                    for use in a.proj[2 * i:2 * i + 2]:
                        wait_emptied(ve, use)
                    link(V.tensor_tensor(sq, area, area, ALU.mult))
                    V.tensor_reduce(ss[:, a.qk_stat[i] % 2, 0:32], sq.rearrange("p (h d) -> p h d", d=HD), X,
                                    ALU.add).then_inc(squared, 1)
                    ve.wait_ge(rs_ready, a.qk_stat[i] + 1)
                    heads = area.rearrange("p (h d) -> p h d", d=HD)
                    last = V.tensor_tensor(heads, heads, spread(rs[:, a.qk_stat[i] % 2, 0:32], 2, HD), ALU.mult)
                last.then_inc(qk_ready, 1)
                feed(2 * a.proj[5].chunk + 5)
                if nth == 0:
                    ve.wait_ge(rel_loaded, 16)
                attention(a.att, P, kT_area, o_area, HD ** -0.5,
                          lambda g, qb: relbias[:, 4 * g:4 * g + 4, P:S] if qb == 0 else relbias[:, 4 * g:4 * g + 4, :],
                          k_scale=head_gain[:, 2 * nth + 1:2 * nth + 2], diff=a.diff,
                          o_stat=a.o_stat if a.diff else None)
                update(a.att.wo[1])

            softmax_layer(plan.moba, 0, 1)
            mlp(plan.mlp1, 1)
            softmax_layer(plan.diff, 1, 2)
            mlp(plan.mlp2, 2)
            retention(plan.ret1, 3)
            mlp(plan.mlp3, 3)


_INS = ["x", "c", "positions", "a_norm_g", "a_w_in", "a_b_f", "a_w_o", "kv_norm_g", "kv_w_mod", "kv_b_mod",
        "kv_w_down", "kv_latent_g", "kv_w_up", "b_norm_g", "b_w_dq", "b_q_norm_g", "b_w_uq", "b_w_o", "w_mod",
        "b_mod", "ffn_norm_g", "router_w", "router_bias", "exp_w_gate", "exp_w_up", "exp_w_down", "final_norm_g",
        "rel_bias_2", "norm1_2", "norm2_2", "w_up_2", "w_down_2", "ret_w_in_2", "ret_w_out_2", "moba_w_in_2",
        "moba_q_norm_2", "moba_k_norm_2", "moba_w_out_2", "diff_w_in_2", "diff_q_norm_2", "diff_k_norm_2",
        "diff_lambda_2", "diff_subln_2", "diff_w_out_2"]


def kernel(**inputs):
    import concourse.bacc as bacc
    from concourse.bass_utils import run_bass_kernel_spmd

    nc = bacc.Bacc("TRN2", target_bir_lowering=False, num_devices=1)
    arrays = {}

    def dram(name, a):
        arrays[name] = a
        return nc.dram_tensor(name, a.shape, mybir.dt.from_np(a.dtype), kind="ExternalInput").ap()

    w = {name: dram(f"in_{name}", np.ascontiguousarray(inputs[name])) for name in _INS}
    table = {name: dram(f"table_{name}", a) for name, a in shape_constants().items()}
    out = nc.dram_tensor("out", (1, S, D), F32, kind="ExternalOutput").ap()
    rel_scratch = nc.dram_tensor("rel_scratch", (HEADS, P, 384), F32, kind="Internal").ap()
    build(nc, w, table, out, rel_scratch)
    return run_bass_kernel_spmd(nc, [arrays], core_ids=[0]).results[0]["out"]
```
